# Optimizing a Trainium2 kernel written in Bass

```python
import jax, jax.numpy as jnp
from jax import lax
import numpy as np

D_MODEL = 1024
BATCH = 1
SEQ = 512
DEPTH = 1
DEC_BATCH = 8
DEC_SEQ = 8
PAST_LEN = 4096
PAGE_SIZE = 128

N_HEADS = 8
HEAD_DIM = 64
D_ATTN = N_HEADS * HEAD_DIM
D_CONV = 512
CONV_W = 31
N_IDX_HEADS = 8
IDX_DIM = 32
TOPK_MAX = 256
D_FF = 2816
ROPE_THETA = 10000.0
EPS = 1e-6
Q_BLOCK = 128
IDX_W_SCALE = (N_IDX_HEADS * IDX_DIM) ** -0.5
SPLIT_SIZES = [D_CONV, D_CONV, D_ATTN, D_ATTN, D_ATTN, N_IDX_HEADS * IDX_DIM, IDX_DIM, N_IDX_HEADS, D_MODEL, D_MODEL]
P_IN = sum(SPLIT_SIZES)
SPLIT_AT = [int(i) for i in np.cumsum(SPLIT_SIZES)[:-1]]

kernel_name = "macaron_conv_dsa_hybrid_step"

def rms_norm(x, g):
    xf = x.astype(jnp.float32)
    y = xf * lax.rsqrt(jnp.mean(xf * xf, axis=-1, keepdims=True) + EPS)
    return (y * g.astype(jnp.float32)).astype(x.dtype)

def layer_norm(x, g, b):
    xf = x.astype(jnp.float32)
    mu = jnp.mean(xf, axis=-1, keepdims=True)
    xc = xf - mu
    y = xc * lax.rsqrt(jnp.mean(xc * xc, axis=-1, keepdims=True) + EPS)
    return (y * g.astype(jnp.float32) + b.astype(jnp.float32)).astype(x.dtype)

def rope(x, pos):
    d = x.shape[-1]
    half = d // 2
    inv = jnp.float32(ROPE_THETA) ** (-jnp.arange(half, dtype=jnp.float32) * (2.0 / d))
    ang = pos.astype(jnp.float32)[:, None] * inv[None, :]
    cos = jnp.cos(ang)[:, None, :]
    sin = jnp.sin(ang)[:, None, :]
    xf = x.astype(jnp.float32)
    x1, x2 = xf[..., :half], xf[..., half:]
    return jnp.concatenate([x1 * cos - x2 * sin, x1 * sin + x2 * cos], axis=-1).astype(x.dtype)

def swiglu_ffn(h, w_in, w_out):
    g, u = jnp.split(h @ w_in, 2, axis=-1)
    return (jax.nn.silu(g) * u) @ w_out

def project_in(h, w_in, g_q, g_k, pos):
    B, T, _ = h.shape
    a_glu, b_glu, q, k, v, qi, ki, wi, gc, ga = jnp.split(h @ w_in, SPLIT_AT, axis=-1)
    u = a_glu * jax.nn.sigmoid(b_glu)
    q = rope(rms_norm(q.reshape(B, T, N_HEADS, HEAD_DIM), g_q), pos)
    k = rope(rms_norm(k.reshape(B, T, N_HEADS, HEAD_DIM), g_k), pos)
    v = v.reshape(B, T, N_HEADS, HEAD_DIM)
    qi = rope(qi.reshape(B, T, N_IDX_HEADS, IDX_DIM), pos)
    ki = rope(ki[:, :, None, :], pos)[:, :, 0, :]
    wi = wi * IDX_W_SCALE
    return u, q, k, v, qi, ki, wi, jax.nn.sigmoid(gc), jax.nn.sigmoid(ga)

def conv_branch(u, prev, w_dw, b_dw, g_ln, b_ln, w_out):
    xp = jnp.concatenate([prev, u], axis=1)
    y = lax.conv_general_dilated(xp, w_dw[:, None, :], (1,), 'VALID',
                                 dimension_numbers=('NWC', 'WIO', 'NWC'),
                                 feature_group_count=D_CONV) + b_dw
    y = jax.nn.silu(layer_norm(y, g_ln, b_ln))
    return y @ w_out, xp[:, -(CONV_W - 1):]

def index_scores(qi, wi, ki):
    dots = jnp.einsum('thd,sd->ths', qi, ki)
    return jnp.einsum('th,ths->ts', wi, jax.nn.relu(dots)).astype(jnp.float32)

def select_keys(scores, qpos, n_keys):
    topk = min(TOPK_MAX, n_keys // 4)
    kpos = jnp.arange(n_keys)
    admissible = kpos[None, :] <= qpos[:, None]
    _, idx = lax.top_k(jnp.where(admissible, scores, -jnp.inf), topk)
    return idx, idx <= qpos[:, None]

def gathered_attention(q, k_sel, v_sel, valid):
    logits = jnp.einsum('thd,tkhd->thk', q, k_sel).astype(jnp.float32) * (HEAD_DIM ** -0.5)
    logits = jnp.where(valid[:, None, :], logits, -jnp.inf)
    p = jax.nn.softmax(logits, axis=-1).astype(v_sel.dtype)
    return jnp.einsum('thk,tkhd->thd', p, v_sel)

def prompt_sparse_attention(q, k, v, qi, ki, wi):
    B, T = q.shape[0], q.shape[1]
    nb = T // Q_BLOCK
    qpos_blocks = jnp.arange(T).reshape(nb, Q_BLOCK)

    def one_sequence(args):
        qs, ks, vs, qis, kis, wis = args

        def one_block(blk):
            qb, qib, wib, qpos = blk
            idx, valid = select_keys(index_scores(qib, wib, kis), qpos, T)
            return gathered_attention(qb, ks[idx], vs[idx], valid)

        out = lax.map(one_block, (qs.reshape(nb, Q_BLOCK, N_HEADS, HEAD_DIM),
                                  qis.reshape(nb, Q_BLOCK, N_IDX_HEADS, IDX_DIM),
                                  wis.reshape(nb, Q_BLOCK, N_IDX_HEADS), qpos_blocks))
        return out.reshape(T, N_HEADS, HEAD_DIM)

    return lax.map(one_sequence, (q, k, v, qi, ki, wi))

def sample_sparse_attention(q, k, v, qi, ki, wi, page_table, pool_k, pool_v, pool_ik):
    T = q.shape[1]
    n_past = page_table.shape[1] * PAGE_SIZE
    qpos = n_past + jnp.arange(T)

    def one_sequence(qs, ks, vs, qis, kis, wis, pt):
        ki_all = jnp.concatenate([pool_ik[pt].reshape(n_past, IDX_DIM), kis], axis=0)
        idx, valid = select_keys(index_scores(qis, wis, ki_all), qpos, n_past + T)
        in_past = (idx < n_past)[..., None, None]
        pidx = jnp.minimum(idx, n_past - 1)
        phys = pt[pidx // PAGE_SIZE]
        off = pidx % PAGE_SIZE
        nidx = jnp.clip(idx - n_past, 0, T - 1)
        k_sel = jnp.where(in_past, pool_k[phys, off], ks[nidx])
        v_sel = jnp.where(in_past, pool_v[phys, off], vs[nidx])
        return gathered_attention(qs, k_sel, v_sel, valid)

    return jax.vmap(one_sequence)(q, k, v, qi, ki, wi, page_table)

def merge_branches(x, conv_out, att, gate_c, gate_a, w_aout, w_o):
    B, T = att.shape[0], att.shape[1]
    a = att.reshape(B, T, D_ATTN) @ w_aout
    return x + (gate_c * conv_out + gate_a * a) @ w_o

def setup_inputs(seed: int = 0) -> dict:
    key = jax.random.key(seed)
    ks = jax.random.split(key, 32)
    n_pages = PAST_LEN // PAGE_SIZE
    n_phys = (DEC_BATCH * n_pages * 5) // 4

    def nrm(k, shape, scale):
        return jax.random.normal(k, shape, jnp.float32) * scale

    def gain(k, shape):
        return 1.0 + 0.05 * jax.random.normal(k, shape, jnp.float32)

    perm = jax.random.permutation(ks[6], n_phys)[:DEC_BATCH * n_pages]
    return {
        "x_prompt": nrm(ks[0], (BATCH, SEQ, D_MODEL), 1.0),
        "x_sample": nrm(ks[1], (DEC_BATCH, DEC_SEQ, D_MODEL), 1.0),
        "cache_k": nrm(ks[2], (DEPTH, n_phys, PAGE_SIZE, N_HEADS, HEAD_DIM), 1.0),
        "cache_v": nrm(ks[3], (DEPTH, n_phys, PAGE_SIZE, N_HEADS, HEAD_DIM), 1.0),
        "cache_idx_k": nrm(ks[4], (DEPTH, n_phys, PAGE_SIZE, IDX_DIM), 1.0),
        "state_conv": nrm(ks[5], (DEPTH, DEC_BATCH, CONV_W - 1, D_CONV), 0.5),
        "page_table": perm.reshape(DEC_BATCH, n_pages).astype(jnp.int32),
        "g_ffn1": gain(ks[7], (DEPTH, D_MODEL)),
        "w_ffn1_in": nrm(ks[8], (DEPTH, D_MODEL, 2 * D_FF), D_MODEL ** -0.5),
        "w_ffn1_out": nrm(ks[9], (DEPTH, D_FF, D_MODEL), D_FF ** -0.5),
        "g_mix": gain(ks[10], (DEPTH, D_MODEL)),
        "w_in": nrm(ks[11], (DEPTH, D_MODEL, P_IN), D_MODEL ** -0.5),
        "g_q": gain(ks[12], (DEPTH, HEAD_DIM)),
        "g_k": gain(ks[13], (DEPTH, HEAD_DIM)),
        "w_dw": nrm(ks[14], (DEPTH, CONV_W, D_CONV), CONV_W ** -0.5),
        "b_dw": nrm(ks[15], (DEPTH, D_CONV), 0.02),
        "g_cln": gain(ks[16], (DEPTH, D_CONV)),
        "b_cln": nrm(ks[17], (DEPTH, D_CONV), 0.02),
        "w_cout": nrm(ks[18], (DEPTH, D_CONV, D_MODEL), D_CONV ** -0.5),
        "w_aout": nrm(ks[19], (DEPTH, D_ATTN, D_MODEL), D_ATTN ** -0.5),
        "w_o": nrm(ks[20], (DEPTH, D_MODEL, D_MODEL), D_MODEL ** -0.5),
        "g_ffn2": gain(ks[21], (DEPTH, D_MODEL)),
        "w_ffn2_in": nrm(ks[22], (DEPTH, D_MODEL, 2 * D_FF), D_MODEL ** -0.5),
        "w_ffn2_out": nrm(ks[23], (DEPTH, D_FF, D_MODEL), D_FF ** -0.5),
    }

def reference(x_prompt, x_sample, cache_k, cache_v, cache_idx_k, state_conv, page_table,
              g_ffn1, w_ffn1_in, w_ffn1_out, g_mix, w_in, g_q, g_k, w_dw, b_dw, g_cln, b_cln,
              w_cout, w_aout, w_o, g_ffn2, w_ffn2_in, w_ffn2_out):
    xp, xs = x_prompt, x_sample
    pos_p = jnp.arange(xp.shape[1])
    pos_s = PAST_LEN + jnp.arange(xs.shape[1])
    kp_l, vp_l, ikp_l, cp_l, ks_l, vs_l, iks_l, cs_l = [], [], [], [], [], [], [], []
    for l in range(DEPTH):
        xp = xp + 0.5 * swiglu_ffn(rms_norm(xp, g_ffn1[l]), w_ffn1_in[l], w_ffn1_out[l])
        xs = xs + 0.5 * swiglu_ffn(rms_norm(xs, g_ffn1[l]), w_ffn1_in[l], w_ffn1_out[l])
        up, qp, kp, vp, qip, kip, wip, gcp, gap = project_in(rms_norm(xp, g_mix[l]), w_in[l], g_q[l], g_k[l], pos_p)
        us, qs, kss, vss, qis, kis, wis, gcs, gas = project_in(rms_norm(xs, g_mix[l]), w_in[l], g_q[l], g_k[l], pos_s)
        conv_p, st_p = conv_branch(up, jnp.zeros((up.shape[0], CONV_W - 1, D_CONV), up.dtype),
                                   w_dw[l], b_dw[l], g_cln[l], b_cln[l], w_cout[l])
        conv_s, st_s = conv_branch(us, state_conv[l], w_dw[l], b_dw[l], g_cln[l], b_cln[l], w_cout[l])
        att_p = prompt_sparse_attention(qp, kp, vp, qip, kip, wip)
        att_s = sample_sparse_attention(qs, kss, vss, qis, kis, wis, page_table,
                                        cache_k[l], cache_v[l], cache_idx_k[l])
        xp = merge_branches(xp, conv_p, att_p, gcp, gap, w_aout[l], w_o[l])
        xs = merge_branches(xs, conv_s, att_s, gcs, gas, w_aout[l], w_o[l])
        xp = xp + 0.5 * swiglu_ffn(rms_norm(xp, g_ffn2[l]), w_ffn2_in[l], w_ffn2_out[l])
        xs = xs + 0.5 * swiglu_ffn(rms_norm(xs, g_ffn2[l]), w_ffn2_in[l], w_ffn2_out[l])
        kp_l.append(kp); vp_l.append(vp); ikp_l.append(kip); cp_l.append(st_p)
        ks_l.append(kss); vs_l.append(vss); iks_l.append(kis); cs_l.append(st_s)
    return (xp, xs, jnp.stack(kp_l), jnp.stack(vp_l), jnp.stack(ikp_l), jnp.stack(cp_l),
            jnp.stack(ks_l), jnp.stack(vs_l), jnp.stack(iks_l), jnp.stack(cs_l))


_drawn_inputs = setup_inputs


def setup_inputs(seed=0):
    import zlib

    import numpy as np

    out = dict(_drawn_inputs(seed))
    spreads = {}
    factors = {'g_q': 8.0, 'b_dw': 4.428, 'g_cln': 3.105, 'b_cln': 8.0, 'g_ffn2': 2.868}
    for name, (base, spread) in spreads.items():
        noise = np.random.default_rng([zlib.crc32(name.encode()), seed]).standard_normal(out[name].shape)
        drawn = base * np.exp(spread * noise) if base else spread * noise
        out[name] = __import__('jax').numpy.asarray(drawn.astype(out[name].dtype))
    for name, factor in factors.items():
        out[name] = (out[name] * factor).astype(out[name].dtype)
    return out
```

```python
from contextlib import ExitStack

import numpy as np

import concourse.bass as bass
from concourse import mybir

ALU = mybir.AluOpType
ACT = mybir.ActivationFunctionType
AX = mybir.AxisListType
F32 = mybir.dt.float32
F32R = mybir.dt.float32r
BF16 = mybir.dt.bfloat16
I32 = mybir.dt.int32

P = 128
D = 1024
SEQ, NSEQ, NEW = 512, 8, 8
NS = NSEQ * NEW
NT = NS + SEQ
HALF = NT // 2
KD = D // P
FF = 2816
KF = FF // P
H, HD = 8, 64
DA = H * HD
KA = DA // P
IH, ID = 8, 32
CW = 31
DC = 512
KC = DC // P
PAGE, NPAGE, NPHYS = 128, 32, 320
PAST = PAGE * NPAGE
TOPK_S, TOPK_P = 256, 128
WIDTH = PAST // 2 + NS
TB = 5
EPS = 1e-6
IDX_SCALE = (IH * ID) ** -0.5
BARRED = -1e38
TAKEN = -3e38
OFF = -1e30
P_IN = 2 * DC + 3 * DA + IH * ID + ID + IH + 2 * D
COL_A, COL_B = 0, DC
COL_Q, COL_K, COL_V = 2 * DC, 2 * DC + DA, 2 * DC + 2 * DA
COL_I = 2 * DC + 3 * DA
NI = IH * ID + ID + IH
COL_GC = COL_I + NI
COL_GA = COL_GC + D


def block_cols(tb):
    return (0, P) if tb == 0 else (NS + P * (tb - 1), NS + P * tb)


def constants():
    c = {}
    p = np.arange(P)
    c["ident"] = np.eye(P, dtype=np.float32)
    pos = np.zeros((P, TB), np.float32)
    pos[:, 0] = np.where(p < NS, PAST + p % NEW, p - NS)
    for tb in range(1, TB):
        pos[:, tb] = P * (tb - 1) + p
    for name, d in (("rope", HD), ("ropei", ID)):
        half = d // 2
        inv = 10000.0 ** (-np.arange(half) * (2.0 / d))
        ang = (pos[:, :, None] * inv.astype(np.float32)[None, None, :]).astype(np.float32)
        c[name] = np.concatenate([np.cos(ang), np.sin(ang)], axis=-1).astype(np.float32)
    r_k4, r_q = p // 64, p % 64 // 8
    m = np.zeros((P, NSEQ, P), np.float32)
    for s in range(NSEQ):
        m[:, s, :] = (r_k4[:, None] == p[None, :] // 64) & (p[None, :] % 64 // 8 == s) & (r_q[:, None] == p[None, :] % 8)
    c["spread"] = m
    c["pair"] = (p[:, None] % 64 == p[None, :] % 64).astype(np.float32)
    c["first"] = ((p[:, None] < 64) & (p[None, :] == p[:, None] + 64)).astype(np.float32)
    t = np.arange(NS)
    c["newmask"] = np.where((t[:, None] // NEW == t[None, :] // NEW) & (t[None, :] <= t[:, None]), 0.0, BARRED).astype(np.float32)
    c["causal"] = np.where(p[None, :] <= p[:, None], 0.0, BARRED).astype(np.float32)
    c["digit"] = np.broadcast_to(np.arange(16, dtype=np.float32)[None, :, None], (P, 16, 8)).copy()
    c["slotno"] = np.broadcast_to(np.arange(TOPK_S, dtype=np.float32), (NS, TOPK_S)).copy()
    c["headmask"] = (p[:, None] % 8 == np.arange(DA)[None, :] // HD).astype(np.float32)
    c["qsel"] = (p[:, None] // 8 == np.arange(16)[None, :]).astype(np.float32)
    c["ownq"] = np.broadcast_to((p[:, None] % 8 == np.arange(8)[None, :])[:, None, :], (P, 32, 8)).astype(np.float32).copy()
    c["pcol"] = p[:, None].astype(np.float32)
    return c


def hybrid_step(nc, inp, con, out):
    ctx = ExitStack()
    with ctx:
        base0 = 16512
        used = {}

        def place(off, items):
            res = []
            for name, shape, dt in items:
                size = int(np.prod(shape[1:])) * (2 if dt == BF16 else 4)
                size = (size + 31) // 32 * 32
                assert off + size <= 229344, (name, off, size)
                res.append(nc.alloc_sbuf_tensor_at(name, list(shape), dt, offset=off))
                used[name] = (off, size)
                off += size
            return res, off

        (xT, h_hi, h_lo, w_raw, w_hi, w_lo, rstd, ident, ones, g1c, gmc, g2c, causal, ptile), arena = place(base0, [
            ("xT", (P, KD, NT), F32), ("h_hi", (P, KD, NT), F32R), ("h_lo", (P, KD, NT), F32R),
            ("w_raw", (P, 2, 1024), F32), ("w_hi", (P, 2, 1024), F32R), ("w_lo", (P, 2, 1024), F32R),
            ("rstd", (P, NT), F32), ("ident", (P, P), F32), ("ones", (P, P), F32),
            ("g1c", (P, KD), F32), ("gmc", (P, KD), F32), ("g2c", (P, KD), F32), ("causal", (P, P), F32),
            ("ptile", (P, 2), I32)])
        (small, ismall, wconv, bconv, gcln, bcln, gqb, gkb, slotbias, nb, slotidx, wv), arena = place(arena, [
            ("small", (P, 64), F32), ("ismall", (P, 8), I32), ("wconv", (P, KC, CW), F32), ("bconv", (P, KC), F32),
            ("gcln", (P, KC), F32), ("bcln", (P, KC), F32), ("gqb", (P, HD), F32), ("gkb", (P, HD), F32),
            ("slotbias", (NS, TOPK_S), F32), ("nb", (NS, NS), F32), ("slotidx", (P, 4, 2), I32), ("wv", (P, NSEQ), F32)])
        (a_hi, a_lo, silu_g, prod_t), _ = place(arena, [
            ("a_hi", (P, KF, NT), F32R), ("a_lo", (P, KF, NT), F32R), ("silu_g", (P, 2, NT), F32), ("prod_t", (P, 2, NT), F32)])
        (sq, hf, xnat), _ = place(arena, [("sq", (P, KD, NT), F32), ("hf", (P, 2, NT), F32), ("xnat", (P, TB, D), F32)])
        (vn, qT, kT, iT, wisc, S, attT, idxT), m1 = place(arena, [
            ("vn", (P, TB, DA), F32), ("qT", (P, KA, NT), F32), ("kT", (P, KA, NT), F32), ("iT", (P, 3, NT), F32),
            ("wisc", (P, TB, IH), F32), ("S", (P, WIDTH), F32), ("attT", (P, KA, NT), F32), ("idxT", (P, 2, NS), I32)])
        (c_hi, c_lo), m2 = place(m1, [("c_hi", (P, KC, NT), F32R), ("c_lo", (P, KC, NT), F32R)])
        (ikn,), _ = place(m1, [("ikn", (P, PAGE * ID), F32)])
        (idxn, iro, qn, kn, rt1, rt2), _ = place(m2, [
            ("idxn", (P, TB, NI), F32), ("iro", (P, TB, 12, ID), F32), ("qn", (P, TB, DA), F32), ("kn", (P, TB, DA), F32),
            ("rt1", (P, TB, H, 32), F32), ("rt2", (P, TB, H, 32), F32)])
        (qrep,), _ = place(used["S"][0], [("qrep", (NS, IH, 4, ID), F32)])
        (ikT, qbd, wst, spread, relud), _ = place(m2, [
            ("ikT", (P, 32, P), F32), ("qbd", (P, NSEQ, 2, P), F32), ("wst", (P, NSEQ, P), F32),
            ("spread", (P, NSEQ, P), F32), ("relud", (P, 2, 512), F32)])
        (U_p, U_s, yacc, sgb, stn, ysq), _ = place(m2, [
            ("U_p", (P, KC, CW - 1 + SEQ), F32), ("U_s", (P, KC, NSEQ, CW - 1 + NEW), F32), ("yacc", (P, KC, NT), F32),
            ("sgb", (P, 2, NT), F32), ("stn", (120, 2, DC), F32), ("ysq", (P, KC, NT), F32)])
        (unat,), _ = place(used["ysq"][0], [("unat", (P, 2, DC), F32)])
        (EQ, CUM, SEL), _ = place(m2, [("EQ", (P, WIDTH), F32), ("CUM", (P, WIDTH), F32), ("SEL", (P, WIDTH), F32)])
        (pairm, firstm, newmask, slotno), lookups = place(used["attT"][0], [
            ("pairm", (P, P), F32), ("firstm", (P, P), F32), ("newmask", (NS, NS), F32), ("slotno", (NS, TOPK_S), F32)])
        (RTi,), _ = place(used["S"][0], [("RTi", (P, 16, P), I32)])
        (adig, bdig, ohA, ohB, ohV, tab, digit, ownq), _ = place(m2, [
            ("adig", (P, 16, P), BF16), ("bdig", (P, 16, P), BF16), ("ohA", (P, NPAGE, 16, 8), BF16),
            ("ohB", (P, NPAGE, 16, 8), BF16), ("ohV", (P, NPAGE, 2, 16, 8), BF16), ("tab", (P, 2, NSEQ, NPAGE, 8), BF16),
            ("digit", (P, 16, 8), BF16), ("ownq", (P, 32, 8), F32)])
        (tmpi,), _ = place(used["ohV"][0], [("tmpi", (P, 16, P), I32)])
        (ptb, diag, rowidx, idxr, digitf, pcol, ptv), e_ = place(lookups, [
            ("ptb", (P, NSEQ * NPAGE), I32), ("diag", (P, 32, 8), F32), ("rowidx", (P, NSEQ, 32), F32),
            ("idxr", (NS, TOPK_S), F32), ("digitf", (P, 16, 8), F32), ("pcol", (P, 1), F32), ("ptv", (P, 2, NSEQ * NPAGE), I32)])
        (kv, pT, pnT, zq, mz, G, qb, kprod), _ = place(m2, [
            ("kv", (P, 4, 2, DA), F32), ("pT", (P, 2, H, NS), F32), ("pnT", (NS, H, NS), F32),
            ("zq", (P, 4, 2, 248), F32), ("mz", (P, DA), F32), ("G", (P, 16, NS), F32), ("qb", (P, 4, DA), F32),
            ("kprod", (P, 2, DA), F32)])
        (L,), _ = place(used["qb"][0], [("L", (NS, H, TOPK_S + NS), F32)])
        (headmask, qsel), _ = place(used["S"][0], [("headmask", (P, DA), F32), ("qsel", (P, 16), F32)])
        (Sp, rp, biasp, Lp, Pp, pTp, m8), _ = place(m2, [
            ("Sp", (P, SEQ), F32), ("rp", (P, 2, SEQ), F32), ("biasp", (P, 4, SEQ), F32), ("Lp", (P, 2, SEQ), F32),
            ("Pp", (P, 2, SEQ), F32), ("pTp", (P, 2, 4, P), F32), ("m8", (P, 8), F32)])
        (t_hi, t_lo), _ = place(used["vn"][0], [("t_hi", (P, KA, NT), F32R), ("t_lo", (P, KA, NT), F32R)])
        (m_hi, m_lo, sg1, sg2), _ = place(m2, [
            ("m_hi", (P, KD, NT), F32R), ("m_lo", (P, KD, NT), F32R), ("sg1", (P, 2, NT), F32), ("sg2", (P, 2, NT), F32)])
        (mc,), _ = place(used["kT"][0], [("mc", (P, 2, NT), F32)])

        assert e_ <= used["attT"][0] + used["attT"][1]
        (ropet, ropei), _ = place(lookups, [("ropet", (P, TB, HD), F32), ("ropei", (P, TB, ID), F32)])

        ps = ctx.enter_context(nc.psum_tensor("ps", [P, 8, 512], F32))
        q_dram = nc.dram_tensor("q_scratch", (NS, DA), F32, kind="Internal").ap()
        wi_dram = nc.dram_tensor("wi_scratch", (NS, IH), F32, kind="Internal").ap()
        idx_dram = nc.dram_tensor("idx_scratch", (16, 8, NSEQ, 16), F32, kind="Internal").ap()

        sems = {}

        def S_(name):
            if name not in sems:
                sems[name] = ctx.enter_context(nc.semaphore(name))
            return sems[name]

        block = ctx.enter_context(nc.Block())

        U_FFN = KD // 4 * 2 * (FF // 256) + 4 * 6
        U1, UA = 0, U_FFN
        UB = UA + 16
        UM = UB + 8
        UO = UM + 24
        U2 = UO + 8
        C_FFN = 11 + 2

        def pair_ps(half, m):
            return ps[:, 4 * half + 2 * m:4 * half + 2 * m + 2, 0:HALF]

        def halves(ap):
            return ap.rearrange("p (h n) -> p h n", h=2)

        win_v = inp["w_in"].rearrange("o (k p) n -> p (o k) n", p=P)

        @block.sync
        def _(sp):
            def load(u, src, slot, n):
                sp.wait_ge(S_("lo_ready"), u + 1)
                sp.sem_inc(S_("load_turn"), 1)
                dst = w_raw[:, slot, 0:n]
                sp.dma_start(dst.rearrange("p (k n) -> p k n", k=src.shape[1]), src).then_inc(S_(f"raw{slot}"), 16)

            def ffn(u0, w1, w2):
                v1 = w1.rearrange("o (k p) n -> p (o k) n", p=P)
                v2 = w2.rearrange("o (k p) n -> p (o k) n", p=P)
                with sp.Fori(0, FF // 256) as i:
                    for j in range(4):
                        load(u0 + 4 * i + j, v1[:, 4 * (j % 2):4 * (j % 2) + 4, bass.ds(i * 256 + (j // 2) * FF, 256)], j % 2, 1024)
                with sp.Fori(0, 2) as i:
                    for j in range(12):
                        k0 = 4 * (j % 6)
                        k1 = min(k0 + 4, KF)
                        load(u0 + 44 + 12 * i + j, v2[:, k0:k1, bass.ds(i * 512 + (j // 6) * 256, 256)], j % 2, (k1 - k0) * 256)

            ffn(U1, inp["w_ffn1_in"], inp["w_ffn1_out"])
            u = UA
            for col, n in ((COL_I, NI), (COL_Q, DA), (COL_K, DA), (COL_V, DA)):
                for j in range(4):
                    load(u, win_v[:, 2 * j:2 * j + 2, col:col + n], u % 2, 2 * n)
                    u += 1
            for pr in range(2):
                for col in (COL_A, COL_B):
                    for j in range(2):
                        load(u, win_v[:, 4 * j:4 * j + 4, col + 256 * pr:col + 256 * pr + 256], u % 2, 1024)
                        u += 1
            sp.wait_ge(S_("idxT_ready"), 1)
            with sp.Fori(0, NS // 4) as i:
                for j in range(4):
                    sp.wait_ge(S_("kv_used"), 4 * i + j + 1)
                    sp.dma_start(qb[:, j, :], q_dram[bass.ds(4 * i + j, 1), :].to_broadcast([P, DA])).then_inc(S_(f"qb{j}"), 16)
            vc = inp["w_cout"].rearrange("o (k p) n -> p (o k) n", p=P)
            va = inp["w_aout"].rearrange("o (k p) n -> p (o k) n", p=P)
            with sp.Fori(0, 4) as i:
                cs = lambda c: bass.ds(i * 256 + c, 256)
                load(UM + 6 * i, win_v[:, 0:4, cs(COL_GC)], 0, 1024)
                load(UM + 6 * i + 1, win_v[:, 4:8, cs(COL_GC)], 1, 1024)
                load(UM + 6 * i + 2, vc[:, :, cs(0)], 0, 1024)
                load(UM + 6 * i + 3, win_v[:, 0:4, cs(COL_GA)], 1, 1024)
                load(UM + 6 * i + 4, win_v[:, 4:8, cs(COL_GA)], 0, 1024)
                load(UM + 6 * i + 5, va[:, :, cs(0)], 1, 1024)
            vo = inp["w_o"].rearrange("o (k p) n -> p (o k) n", p=P)
            with sp.Fori(0, 4) as i:
                for j in range(2):
                    load(UO + 2 * i + j, vo[:, 4 * j:4 * j + 4, bass.ds(i * 256, 256)], j, 1024)
            ffn(U2, inp["w_ffn2_in"], inp["w_ffn2_out"])
            for tb in range(TB):
                sp.wait_ge(S_("y_ready"), 2 * (tb + 1))
                dst = out["y_sample"] if tb == 0 else out["y_prompt"][P * (tb - 1):P * tb]
                sp.dma_start(dst, xnat[0:NS if tb == 0 else P, tb, :]).then_inc(S_("y_out"), 16)
            sp.wait_ge(S_("y_out"), 16 * TB)

        @block.tensor
        def _(pe):
            turns = [0]

            def turn(mm):
                turns[0] += 1
                mm.then_inc(S_("row_tile_done"), 1)
                pe.wait_ge(S_("row_tile_done"), turns[0])

            def unit(u, slot, x_hi, x_lo, kc0, nk, half, first, last):
                pe.wait_ge(S_("lo_ready"), u + 3)
                hi = w_hi[:, slot, 0:nk * 256].rearrange("p (k n) -> p k n", k=nk)
                lo = w_lo[:, slot, 0:nk * 256].rearrange("p (k n) -> p k n", k=nk)
                for m in range(2):
                    for k in range(nk):
                        for w, x, fst in ((hi, x_hi, True), (hi, x_lo, False), (lo, x_hi, False)):
                            for hf_ in range(2):
                                mm = pe.matmul(ps[:, 4 * half + 2 * m + hf_, 0:HALF], w[:, k, m * P:(m + 1) * P],
                                               x[:, kc0 + k, hf_ * HALF:(hf_ + 1) * HALF],
                                               start=(first and k == 0 and fst), stop=(last and k == nk - 1 and w is lo))
                mm.then_inc(S_("unit_used"), 1)

            def norm_sums(n):
                for k in range(KD):
                    pe.wait_ge(S_("sq_ready"), KD * n + k + 1)
                    for hf_ in range(2):
                        mm = pe.matmul(ps[:, hf_, 0:HALF], ones[:, :], sq[:, k, hf_ * HALF:(hf_ + 1) * HALF],
                                       start=(k == 0), stop=(k == KD - 1))
                mm.then_inc(S_("sums_ready"), 1)

            def ffn(f, u0, ping0, pong0, hbase):
                pe.wait_ge(S_("h_ready"), hbase + KD)
                with pe.Fori(0, FF // 256) as i:
                    pe.wait_ge(S_("ping_free"), i + (ping0 + 1))
                    for j in range(4):
                        if j == 2:
                            pe.wait_ge(S_("pong_free"), i + (pong0 + 1))
                        unit(4 * i + (u0 + j), j % 2, h_hi, h_lo, 4 * (j % 2), 4, j // 2, j % 2 == 0, j % 2 == 1)
                pe.wait_ge(S_("act_ready"), KF * (f + 1))
                with pe.Fori(0, 2) as i:
                    for j in range(12):
                        if j == 0:
                            pe.wait_ge(S_("ping_free"), i + (ping0 + 12))
                        if j == 6:
                            pe.wait_ge(S_("pong_free"), i + (pong0 + 12))
                        k0 = 4 * (j % 6)
                        unit(12 * i + (u0 + 44 + j), j % 2, a_hi, a_lo, k0, min(4, KF - k0), j // 6, j % 6 == 0, j % 6 == 5)

            pe.wait_ge(S_("const_in"), 16)
            for tb in range(TB):
                pe.wait_ge(S_(f"x_in{tb}"), 16)
                n = NS if tb == 0 else P
                for g in range(2):
                    f = 2 * tb + g
                    if f >= 2:
                        pe.wait_ge(S_("xt_evac"), f - 1)
                    for j in range(4):
                        mm = pe.transpose(ps[:, f % 2, j * n:(j + 1) * n], xnat[0:n, tb, (4 * g + j) * P:(4 * g + j + 1) * P],
                                          ident[0:n, 0:n])
                    mm.then_inc(S_("xt_done"), 1)
            pe.wait_ge(S_("ones_ready"), 1)
            norm_sums(0)
            ffn(0, U1, 0, 0, 0)
            norm_sums(1)
            pe.wait_ge(S_("h_ready"), 2 * KD)
            u = UA
            for g, n in enumerate((NI, DA, DA, DA)):
                for j in range(4):
                    pe.wait_ge(S_("lo_ready"), u + 3)
                    hi = w_hi[:, u % 2, 0:2 * n].rearrange("p (k n) -> p k n", k=2)
                    lo = w_lo[:, u % 2, 0:2 * n].rearrange("p (k n) -> p k n", k=2)
                    for tb in range(TB):
                        s = TB * g + tb
                        if j == 0 and s >= 8:
                            pe.wait_ge(S_("nat_evac"), s - 7)
                        c0, c1 = block_cols(tb)
                        for k in range(2):
                            kk = 2 * j + k
                            pe.matmul(ps[:, s % 8, 0:n], h_hi[:, kk, c0:c1], hi[:, k, :], start=(kk == 0), stop=False)
                            pe.matmul(ps[:, s % 8, 0:n], h_lo[:, kk, c0:c1], hi[:, k, :], start=False, stop=False)
                            mm = pe.matmul(ps[:, s % 8, 0:n], h_hi[:, kk, c0:c1], lo[:, k, :], start=False, stop=(kk == KD - 1))
                        if j == 3 and tb < TB - 1:
                            mm.then_inc(S_("nat_done"), 1)
                    mm.then_inc(S_("unit_used"), 1)
                    u += 1
            pe.wait_ge(S_("nat_evac"), 4 * TB)
            pe.wait_ge(S_("iro_ready"), 1)
            for tb in range(TB):
                n = NS if tb == 0 else P
                if tb >= 2:
                    pe.wait_ge(S_("iT_evac"), tb - 1)
                for j in range(3):
                    mm = pe.transpose(ps[:, tb % 2, j * n:(j + 1) * n], iro[0:n, tb, 4 * j:4 * j + 4, :].rearrange("p a b -> p (a b)"), ident[0:n, 0:n])
                mm.then_inc(S_("iT_done"), 1)
            pe.wait_ge(S_("iT_evac"), TB)
            for w, src in enumerate((qn, kn)):
                pe.wait_ge(S_("qk_ready"), w + 1)
                for tb in range(TB):
                    n = NS if tb == 0 else P
                    f = TB * w + tb
                    if f >= 4:
                        pe.wait_ge(S_("qkT_evac"), f - 3)
                    for j in range(KA):
                        mm = pe.transpose(ps[:, f % 4, j * n:(j + 1) * n], src[0:n, tb, j * P:(j + 1) * P], ident[0:n, 0:n])
                    mm.then_inc(S_("qkT_done"), 1)
            pe.wait_ge(S_("qrep_ready"), 1)
            pe.wait_ge(S_("qkT_evac"), 2 * TB)
            for h in range(IH):
                mm = pe.transpose(ps[:, 4, h * NS:(h + 1) * NS], qrep[:, h, :, :].rearrange("p a b -> p (a b)"), ident[0:NS, 0:NS])
            mm.then_inc(S_("qrepT_done"), 1)
            n_tr = 0
            n_dot = 0

            def scores_w(i):
                s, hp = i // 4, i % 4
                pe.wait_ge(S_("relu_ready"), i + 1)
                mm = pe.matmul(ps[:, hp, :], wst[:, s, :], relud[:, i % 2, :], start=(s == 0), stop=(s == NSEQ - 1))
                mm.then_inc(S_("scores_done"), 1)

            for gseq in range(2):
                pe.wait_ge(S_(f"ik_in{gseq}"), 16)
                for f in range(8):
                    if n_tr >= 2:
                        pe.wait_ge(S_("ikT_evac"), n_tr - 1)
                    for j in range(4):
                        kg = 4 * f + j
                        mm = pe.transpose(ps[:, 6 + n_tr % 2, j * P:(j + 1) * P], ikn[:, kg * P:(kg + 1) * P], ident[:, :])
                    mm.then_inc(S_("ikT_done"), 1)
                    n_tr += 1
                pe.wait_ge(S_("ikT_evac"), n_tr)
                if gseq == 0:
                    pe.wait_ge(S_("qbd_ready"), 1)
                for s4 in range(4):
                    for hp in range(4):
                        s = 4 * gseq + s4
                        if n_dot >= 2:
                            pe.wait_ge(S_("relu_ready"), n_dot - 1)
                        c0 = s4 * 32 + (hp // 2) * 16
                        pe.matmul(ps[:, 4 + n_dot % 2, :], qbd[:, s, hp % 2, :], ikT[:, :, c0:c0 + 16], start=True, stop=True)\
                            .then_inc(S_("dots_done"), 1)
                        if n_dot >= 1:
                            scores_w(n_dot - 1)
                        n_dot += 1
            scores_w(n_dot - 1)
            pe.wait_ge(S_("relu_ready"), n_dot)
            for r in range(0, P, 32):
                for h in (r // 32, r // 32 + 4):
                    mm = pe.matmul(ps[0:NS, 6, h * NS:(h + 1) * NS], iT[r:r + 32, h // 4, 0:NS], iT[r:r + 32, 2, 0:NS], start=(h == 0), stop=True,
                                   skip_group_check=True)
                if r < 96:
                    turn(mm)
            mm.then_inc(S_("newdots_done"), 1)
            pe.wait_ge(S_("S_ready"), 1)
            u = UB
            for pr in range(2):
                if pr == 1:
                    pe.wait_ge(S_("u_ready"), 2)
                for half in range(2):
                    for j in range(2):
                        unit(u, u % 2, h_hi, h_lo, 4 * j, 4, half, j == 0, j == 1)
                        u += 1
            pe.wait_ge(S_("u_ready"), 4)
            pe.wait_ge(S_("state_in"), 16 * 2)
            for b in range(2):
                for j in range(KC):
                    mm = pe.transpose(ps[:, b, j * 120:(j + 1) * 120], stn[:, b, j * P:(j + 1) * P], ident[0:120, 0:120])
                mm.then_inc(S_("st_done"), 1)
            for j in range(KC):
                pe.transpose(ps[0:P, 2, j * P:(j + 1) * P], U_p[:, j, CW - 1 + SEQ - P:CW - 1 + SEQ], ident[:, :])
            for j in range(KC):
                pe.wait_ge(S_("us_packed"), 1)
                mm = pe.transpose(ps[0:NS, 3, j * P:(j + 1) * P], yacc[:, j, 0:NS], ident[:, :])
            mm.then_inc(S_("unat_done"), 1)
            for st in range(2):
                for k in range(KC):
                    pe.wait_ge(S_("ln_in"), KC * st + k + 1)
                    for hf_ in range(2):
                        mm = pe.matmul(ps[:, 4 + 2 * st + hf_, 0:HALF], ones[:, :], (ysq if st else yacc)[:, k, hf_ * HALF:(hf_ + 1) * HALF],
                                       start=(k == 0), stop=(k == KC - 1))
                mm.then_inc(S_("ln_sums"), 1)
            pe.wait_ge(S_("sel_in"), 16 * 2)
            pe.wait_ge(S_("cnt_ready"), 1)
            pe.matmul(ps[:, 7, 0:1], pairm[:, :], small[:, 0:1], start=True, stop=True).then_inc(S_("tot_ready"), 1)
            with pe.Fori(0, 31) as i:
                pe.wait_ge(S_("cnt_ready"), i + 2)
                pe.matmul(ps[:, 7, 0:1], pairm[:, :], small[:, 0:1], start=True, stop=True).then_inc(S_("tot_ready"), 1)
            pe.wait_ge(S_("cnt_ready"), 33)
            pe.matmul(ps[:, 7, 0:1], pairm[:, :], small[:, 1:2], start=True, stop=False)
            pe.matmul(ps[:, 7, 0:1], firstm[:, :], small[:, 2:3], start=False, stop=True).then_inc(S_("tot_ready"), 1)
            pe.wait_ge(S_("cnt_ready"), 34)
            pe.matmul(ps[:, 7, 0:1], firstm[:, :], small[:, 4:5], start=True, stop=True).then_inc(S_("tot_ready"), 1)
            pe.wait_ge(S_("rank_ready"), 1)
            for c in range(16):
                mm = pe.transpose(ps[:, c // 4, (c % 4) * P:(c % 4 + 1) * P], CUM[:, c * P:(c + 1) * P], ident[:, :])
                if c % 4 == 3:
                    mm.then_inc(S_("rankT_done"), 1)
            for s in range(NSEQ):
                pe.wait_ge(S_("onehot_ready"), s + 1)
                for pg in range(NPAGE):
                    mm = pe.matmul(ps[:, 5 + s % 2, 0:256], ohA[:, pg, :, :].rearrange("p a b -> p (a b)"),
                                   ohV[:, pg, :, :, :].rearrange("p v a b -> p (v a b)"), start=(pg == 0), stop=(pg == NPAGE - 1))
                mm.then_inc(S_("slots_done"), 1)
            pe.wait_ge(S_("idx_back"), 16 * NSEQ)
            for c in range(2):
                mm = pe.transpose(ps[:, 6, c * NS:(c + 1) * NS], idxr[:, c * P:(c + 1) * P], ident[0:NS, 0:NS])
            mm.then_inc(S_("idxT_done"), 1)
            for r in (0, 64):
                for h in range(r // 64, H, 2):
                    mm = pe.matmul(ps[0:NS, 4, h * NS:(h + 1) * NS], qT[r:r + 64, h // 2, 0:NS], kT[r:r + 64, h // 2, 0:NS], start=(h == 0), stop=True,
                                   skip_group_check=True)
                turn(mm)
            pe.wait_ge(S_("logits_ready"), NS + 1)
            for h in range(H):
                for c in range(2):
                    mm = pe.transpose(ps[0:NS, h // 2, (h % 2) * 256 + c * P:(h % 2) * 256 + (c + 1) * P], G[:, c * H + h, :], ident[:, :])
            mm.then_inc(S_("logitsT_done"), 1)
            pe.wait_ge(S_("probs_ready"), 1)
            for c in range(2):
                for h in range(H):
                    pe.transpose(ps[:, 5 + c, h * NS:(h + 1) * NS], L[:, h, c * P:(c + 1) * P], ident[0:NS, 0:NS])
            for h in range(H):
                mm = pe.transpose(ps[0:NS, 7, h * NS:(h + 1) * NS], L[:, h, TOPK_S:TOPK_S + NS], ident[0:NS, 0:NS])
            mm.then_inc(S_("probsT_done"), 1)
            pe.wait_ge(S_("probsT_evac"), 2)
            for h in range(H):
                r = 64 * (h % 2)
                mm = pe.matmul(ps[r:r + 64, 5, (h // 2) * NS:(h // 2 + 1) * NS], vn[0:NS, 0, h * HD:(h + 1) * HD], pnT[:, h, :],
                               start=(h < 2), stop=True, skip_group_check=True)
            with pe.Fori(0, 4) as g:
                for qi in range(16):
                    j = qi % 4
                    pe.wait_ge(S_(f"kv_in{j}"), 32 * (16 + 4 * g + qi // 4 + 1))
                    pe.wait_ge(S_("zq_ready"), 16 * g + (qi + 1))
                    if qi == 0:
                        pe.wait_ge(S_("mz_ready"), g + 1)
                    for c in range(2):
                        mm = pe.matmul(ps[:, 0, :], zq[:, j, c, 120 - 8 * qi:248 - 8 * qi], kv[:, j, c, :],
                                       start=(qi == 0 and c == 0), stop=(qi == 15 and c == 1))
                    mm.then_inc(S_("pv_used"), 1)
                pe.wait_ge(S_("mz_ready"), g + 2)
                for hp in range(KA):
                    mm = pe.matmul(ps[:, 4, bass.ds(16 * g + hp * NS, 16)], mz[:, hp * P:(hp + 1) * P], qsel[:, :],
                                   start=True, stop=True, skip_group_check=True)
                mm.then_inc(S_("att_group"), 1)
            pe.wait_ge(S_("atts_evac"), 1)
            n = 0
            for b in range(1, 4):
                nk = P * (b + 1)
                for h in range(IH):
                    if n >= 2:
                        pe.wait_ge(S_("prelu_ready"), n - 1)
                    r = 32 * (h % 4)
                    pe.matmul(ps[:, n % 2, 0:nk], iT[r:r + 32, h // 4, NS + P * b:NS + P * (b + 1)], iT[r:r + 32, 2, NS:NS + nk],
                              start=True, stop=True).then_inc(S_("pdots_done"), 1)
                    n += 1
            pe.wait_ge(S_("prelu_ready"), n)
            steps = [(b, h) for b in range(4) for h in range(H)]

            def plogits(i):
                b, h = steps[i]
                r = 64 * (h % 2)
                if i >= 2:
                    pe.wait_ge(S_("plog_used"), i - 1)
                pe.matmul(ps[:, i % 2, 0:P * (b + 1)], qT[r:r + 64, h // 2, NS + P * b:NS + P * (b + 1)], kT[r:r + 64, h // 2, NS:NS + P * (b + 1)],
                          start=True, stop=True).then_inc(S_("plog_done"), 1)

            def pturn(i):
                b, h = steps[i]
                pe.wait_ge(S_("pprob_ready"), i + 1)
                if i >= 2:
                    pe.wait_ge(S_("pturn_evac"), i - 1)
                for kb in range(b + 1):
                    mm = pe.transpose(ps[:, 2 + i % 2, kb * P:(kb + 1) * P], Pp[:, i % 2, kb * P:(kb + 1) * P], ident[:, :])
                mm.then_inc(S_("pturn_done"), 1)

            def pvalue(i):
                b, h = steps[i]
                r = 64 * (h % 2)
                pe.wait_ge(S_("pturn_evac"), i + 1)
                if i >= 4:
                    pe.wait_ge(S_("patt_evac"), i // 2 - 1)
                for kb in range(b + 1):
                    mm = pe.matmul(ps[r:r + 64, 4 + i // 2 % 2, 0:P], vn[:, kb + 1, h * HD:(h + 1) * HD], pTp[:, i % 2, kb, :],
                                   start=(kb == 0), stop=(kb == b))
                mm.then_inc(S_("patt_done"), 1)

            for i in range(len(steps) + 2):
                if i < len(steps):
                    plogits(i)
                if 1 <= i <= len(steps):
                    pturn(i - 1)
                if i >= 2:
                    pvalue(i - 2)
            pe.wait_ge(S_("patt_evac"), 16)
            pe.wait_ge(S_("t_ready"), KA)
            with pe.Fori(0, 4) as i:
                pe.wait_ge(S_("mping_free"), 2 * i + 1)
                unit(6 * i + UM, 0, h_hi, h_lo, 0, 4, 0, True, False)
                unit(6 * i + (UM + 1), 1, h_hi, h_lo, 4, 4, 0, False, True)
                pe.wait_ge(S_("mpong_free"), 2 * i + 1)
                unit(6 * i + (UM + 2), 0, c_hi, c_lo, 0, 4, 1, True, True)
                pe.wait_ge(S_("mping_free"), 2 * i + 2)
                unit(6 * i + (UM + 3), 1, h_hi, h_lo, 0, 4, 0, True, False)
                unit(6 * i + (UM + 4), 0, h_hi, h_lo, 4, 4, 0, False, True)
                pe.wait_ge(S_("mpong_free"), 2 * i + 2)
                unit(6 * i + (UM + 5), 1, t_hi, t_lo, 0, 4, 1, True, True)
            pe.wait_ge(S_("m_ready"), KD + 1)
            with pe.Fori(0, 2) as i:
                for half in range(2):
                    pe.wait_ge(S_("o_free"), 2 * i + (half + 1))
                    unit(4 * i + (UO + 2 * half), 0, m_hi, m_lo, 0, 4, half, True, False)
                    unit(4 * i + (UO + 2 * half + 1), 1, m_hi, m_lo, 4, 4, half, False, True)
            norm_sums(2)
            ffn(1, U2, C_FFN, C_FFN, 2 * KD)
            pe.wait_ge(S_("pong_free"), 2 * C_FFN + 1)
            for tb in range(TB):
                n = NS if tb == 0 else P
                c0 = 0 if tb == 0 else NS + P * (tb - 1)
                for g in range(2):
                    f = 2 * tb + g
                    if f >= 2:
                        pe.wait_ge(S_("y_ready"), f - 1)
                    for j in range(4):
                        mm = pe.transpose(ps[0:n, f % 2, j * P:(j + 1) * P], xT[:, 4 * g + j, c0:c0 + n], ident[:, :])
                    mm.then_inc(S_("y_done"), 1)

        @block.scalar
        def _(act):
            own = [0]

            def link(ins):
                own[0] += 1
                ins.then_inc(S_("act_own"), 1)

            def settle():
                act.wait_ge(S_("act_own"), own[0])

            def split_hi(u, slot, n=1024, k=None):
                act.wait_ge(S_(f"raw{slot}"), 16 * (k + 1))
                act.wait_ge(S_("unit_used"), u + 1)
                act.activation(w_hi[:, slot, 0:n], w_raw[:, slot, 0:n], ACT.Copy).then_inc(S_("hi_ready"), 1)

            def squares(n):
                for k in range(KD):
                    act.activation(sq[:, k, :], xT[:, k, :], ACT.Square).then_inc(S_("sq_ready"), 1)

            def root(n):
                act.wait_ge(S_("ms_ready"), n + 1)
                act.activation(rstd[:, :], rstd[:, :], ACT.Sqrt).then_inc(S_("root_ready"), 1)

            def ffn(u0, ping0, f):
                with act.Fori(0, FF // 256) as i:
                    h0 = u0 // 2
                    split_hi(4 * i + (u0 + 1), 1, k=2 * i + h0)
                    split_hi(4 * i + (u0 + 2), 0, k=2 * i + (h0 + 1))
                    act.wait_ge(S_("unit_used"), 4 * i + (u0 + 4))
                    act.wait_ge(S_("prod_taken"), 2 * i + (22 * f + 1))
                    for m in range(2):
                        ins = act.activation(halves(silu_g[:, m, :]), pair_ps(0, m), ACT.Silu)
                        ins.then_inc(S_("silu_ready" if m == 0 else "ping_free"), 1)
                    split_hi(4 * i + (u0 + 3), 1, k=2 * i + (h0 + 1))
                    split_hi(4 * i + (u0 + 4), 0, k=2 * i + (h0 + 2))
                for i in range(2):
                    h0 = u0 // 2 + 22
                    for j in range(1, 13):
                        if f == 0 or i == 0 or j < 12:
                            split_hi(12 * i + (u0 + 44 + j), j % 2, n=512 if j % 6 == 5 else 1024, k=6 * i + (h0 + j // 2))

            act.dma_start(ident[:, :], con["ident"]).then_inc(S_("const_in"), 16)
            for tb in range(TB):
                n = NS if tb == 0 else P
                src = inp["x_sample"] if tb == 0 else inp["x_prompt"][P * (tb - 1):P * tb]
                act.dma_start(xnat[0:n, tb, :], src).then_inc(S_(f"x_in{tb}"), 16)
            for dst, name in ((g1c, "g_ffn1"), (gmc, "g_mix"), (g2c, "g_ffn2")):
                act.dma_start(dst[:, :], inp[name].rearrange("o (k p) -> p (o k)", p=P), allow_slow_non_contiguous=True).then_inc(S_("gain_in"), 16)
            act.dma_start(causal[:, :], con["causal"]).then_inc(S_("gain_in"), 16)
            for k in range(KC):
                act.dma_start(wconv[:, k, :], inp["w_dw"][0, :, k * P:(k + 1) * P].rearrange("w p -> p w"), allow_slow_non_contiguous=True)\
                    .then_inc(S_("gain_in"), 16)
            for dst, name in ((bconv, "b_dw"), (gcln, "g_cln"), (bcln, "b_cln")):
                act.dma_start(dst[:, :], inp[name].rearrange("o (k p) -> p (o k)", p=P), allow_slow_non_contiguous=True).then_inc(S_("gain_in"), 16)
            for dst, name in ((gqb, "g_q"), (gkb, "g_k")):
                act.dma_start(dst[:, :], inp[name].to_broadcast([P, HD])).then_inc(S_("gain_in"), 16)
            act.dma_start(ptile[:, :], inp["page_table"].rearrange("(g s) n -> (s n) g", g=2), allow_slow_non_contiguous=True).then_inc(S_("gain_in"), 16)
            split_hi(0, 0, k=0)
            for f in range(2 * TB):
                tb, g = f // 2, f % 2
                n = NS if tb == 0 else P
                c0 = 0 if tb == 0 else NS + P * (tb - 1)
                act.wait_ge(S_("xt_done"), f + 1)
                act.activation(xT[:, 4 * g:4 * g + 4, c0:c0 + n], ps[:, f % 2, 0:4 * n].rearrange("p (j n) -> p j n", j=4), ACT.Copy)\
                    .then_inc(S_("xt_evac"), 1)
            act.wait_ge(S_("xt_evac"), 2 * TB)
            squares(0)
            root(0)
            ffn(U1, 0, 0)
            act.wait_ge(S_("ping_free"), C_FFN + 1)
            act.wait_ge(S_("pong_free"), C_FFN + 1)
            squares(1)
            root(1)
            u = UA
            for g, (dst, n) in enumerate(((idxn, NI), (qn, DA), (kn, DA), (vn, DA))):
                nxt = 2 * n if g else 2 * NI
                for j in range(1, 5):
                    size = 2 * n if j < 4 else (2 * DA if g < 3 else 1024)
                    split_hi(u + j, (u + j) % 2, n=size, k=(u + j) // 2)
                for tb in range(TB):
                    if tb < TB - 1:
                        act.wait_ge(S_("nat_done"), 4 * g + tb + 1)
                    else:
                        act.wait_ge(S_("unit_used"), u + 6)
                    act.activation(dst[:, tb, :], ps[:, (TB * g + tb) % 8, 0:n], ACT.Copy).then_inc(S_("nat_evac"), 1)
                u += 4
            for tb in range(TB):
                n = NS if tb == 0 else P
                c0 = 0 if tb == 0 else NS + P * (tb - 1)
                act.wait_ge(S_("iT_done"), tb + 1)
                act.activation(iT[:, :, c0:c0 + n], ps[:, tb % 2, 0:3 * n].rearrange("p (j n) -> p j n", j=3), ACT.Copy)\
                    .then_inc(S_("iT_evac"), 1)
            for w in range(2):
                act.wait_ge(S_("qkms_ready"), w + 1)
                act.activation(small[:, 8:8 + TB * H], small[:, 8:8 + TB * H], ACT.Sqrt).then_inc(S_("qkroot_ready"), 1)
            for f in range(2 * TB):
                w, tb = f // TB, f % TB
                n = NS if tb == 0 else P
                c0 = 0 if tb == 0 else NS + P * (tb - 1)
                act.wait_ge(S_("qkT_done"), f + 1)
                act.activation((kT if w else qT)[:, :, c0:c0 + n], ps[:, f % 4, 0:4 * n].rearrange("p (j n) -> p j n", j=4), ACT.Copy)\
                    .then_inc(S_("qkT_evac"), 1)
            nt, nd = 0, 0
            for gseq in range(2):
                if gseq == 1:
                    act.wait_ge(S_("dots_done"), 16)
                for f in range(8):
                    act.wait_ge(S_("ikT_done"), nt + 1)
                    if nt == 0:
                        act.wait_ge(S_("nat_stored"), 1)
                    act.activation(ikT[:, 4 * f:4 * f + 4, :], ps[:, 6 + nt % 2, :].rearrange("p (a n) -> p a n", a=4), ACT.Copy)\
                        .then_inc(S_("ikT_evac"), 1)
                    nt += 1
                for i in range(16):
                    act.wait_ge(S_("dots_done"), nd + 1)
                    if nd >= 2:
                        act.wait_ge(S_("scores_done"), nd - 1)
                    act.activation(relud[:, nd % 2, :], ps[:, 4 + nd % 2, :], ACT.Relu).then_inc(S_("relu_ready"), 1)
                    nd += 1
            u = UB
            for pr in range(2):
                split_hi(u + 1, 1, k=(u + 1) // 2)
                split_hi(u + 2, 0, k=(u + 2) // 2)
                split_hi(u + 3, 1, k=(u + 3) // 2)
                if pr == 0:
                    split_hi(u + 4, 0, k=(u + 4) // 2)
                act.wait_ge(S_("unit_used"), u + 6)
                if pr == 1:
                    act.wait_ge(S_("u_ready"), 2)
                for m in range(2):
                    act.activation(halves(sgb[:, m, :]), pair_ps(1, m), ACT.Sigmoid).then_inc(S_("sgb_ready"), 1)
                u += 4
            for b in range(2):
                act.wait_ge(S_("st_done"), b + 1)
                for j in range(KC):
                    act.activation(U_s[:, j, 4 * b:4 * b + 4, 0:CW - 1], ps[:, b, j * 120:(j + 1) * 120].rearrange("p (s t) -> p s t", s=4),
                                   ACT.Copy).then_inc(S_("us_state"), 1)
            act.wait_ge(S_("unat_done"), 1)
            act.activation(unat[:, 0, :], ps[:, 2, :], ACT.Copy).then_inc(S_("unat_evac0"), 1)
            act.activation(unat[0:NS, 1, :], ps[0:NS, 3, :], ACT.Copy).then_inc(S_("unat_evac"), 1)
            act.wait_ge(S_("unat_out"), 32)
            for k in range(KC):
                act.wait_ge(S_("xc_ready"), k + 1)
                act.activation(ysq[:, k, :], yacc[:, k, :], ACT.Square).then_inc(S_("ln_in"), 1)
            act.wait_ge(S_("lnvar_ready"), 1)
            act.activation(rstd[:, :], rstd[:, :], ACT.Sqrt).then_inc(S_("lnroot_ready"), 1)
            for k in range(KC):
                act.wait_ge(S_("z_ready"), k + 1)
                act.activation(yacc[:, k, :], yacc[:, k, :], ACT.Silu, bias=bcln[:, k:k + 1]).then_inc(S_("swish_ready"), 1)
            act.wait_ge(S_("shift_ready"), 1)
            act.activation(L[:, :, :], L[:, :, :], ACT.Exp, scale=HD ** -0.5).then_inc(S_("exp_ready"), 1)
            act.wait_ge(S_("probsT_done"), 1)
            act.activation(pT[:, :, :, :], ps[:, 5:7, :].rearrange("p c (h q) -> p c h q", h=H), ACT.Copy).then_inc(S_("probsT_evac"), 1)
            act.activation(pnT[:, :, :], ps[0:NS, 7, :].rearrange("p (h q) -> p h q", h=H), ACT.Copy).then_inc(S_("probsT_evac"), 1)
            act.wait_ge(S_("probsT_evac"), 2)
            act.wait_ge(S_("zq_zero"), 1)
            with act.Fori(0, NS // 4) as i:
                for j in range(4):
                    act.wait_ge(S_("pv_used"), 4 * i + (j + 1))
                    act.activation(zq[:, j, :, 120:128], pT[:, :, :, bass.ds(4 * i + j, 1)].rearrange("p c h o -> p c (h o)"), ACT.Copy)\
                        .then_inc(S_("zq_ready"), 1)
            for n in range(24):
                b = 1 + n // 8
                nk = P * (b + 1)
                act.wait_ge(S_("pdots_done"), n + 1)
                if n >= 2:
                    act.wait_ge(S_("pscore_used"), n - 1)
                act.activation(rp[:, n % 2, 0:nk], ps[:, n % 2, 0:nk], ACT.Relu).then_inc(S_("prelu_ready"), 1)
            def pexp(i):
                b = i // H
                nk = P * (b + 1)
                act.wait_ge(S_("plog_used"), i + 1)
                if i >= 2:
                    act.wait_ge(S_("pturn_done"), i - 1)
                act.activation(Pp[:, i % 2, 0:nk], Lp[:, i % 2, 0:nk], ACT.Exp, scale=-1.0, bias=small[:, 56 + i % 2:57 + i % 2],
                               accum_out=small[:, 58 + i % 2:59 + i % 2]).then_inc(S_("pexp_ready"), 1)

            def pevac(i):
                b = i // H
                act.wait_ge(S_("pturn_done"), i + 1)
                if i >= 2:
                    act.wait_ge(S_("patt_done"), i - 1)
                act.activation(pTp[:, i % 2, 0:b + 1, :], ps[:, 2 + i % 2, 0:P * (b + 1)].rearrange("p (a n) -> p a n", n=P), ACT.Copy)\
                    .then_inc(S_("pturn_evac"), 1)

            def pout(i):
                b, hp = i // 8, (i % 8) // 2
                act.wait_ge(S_("patt_done"), i + 1)
                act.activation(attT[:, hp, NS + P * b:NS + P * (b + 1)], ps[:, 4 + i // 2 % 2, 0:P], ACT.Copy).then_inc(S_("patt_evac"), 1)

            for i in range(34):
                if i < 32:
                    pexp(i)
                if 1 <= i <= 32:
                    pevac(i - 1)
                if i >= 2 and (i - 2) % 2 == 1:
                    pout(i - 2)
            h0 = UM // 2
            split_hi(UM, 0, k=h0)
            with act.Fori(0, 4) as i:
                split_hi(6 * i + (UM + 1), 1, k=3 * i + h0)
                split_hi(6 * i + (UM + 2), 0, k=3 * i + (h0 + 1))
                act.wait_ge(S_("unit_used"), 6 * i + (UM + 4))
                act.wait_ge(S_("m_ready"), 2 * i + 1)
                for m in range(2):
                    act.activation(halves(sg1[:, m, :]), pair_ps(0, m), ACT.Sigmoid).then_inc(S_("sg1_ready" if m == 0 else "mping_free"), 1)
                split_hi(6 * i + (UM + 3), 1, k=3 * i + (h0 + 1))
                split_hi(6 * i + (UM + 4), 0, k=3 * i + (h0 + 2))
                split_hi(6 * i + (UM + 5), 1, k=3 * i + (h0 + 2))
                act.wait_ge(S_("unit_used"), 6 * i + (UM + 7))
                for m in range(2):
                    act.activation(halves(sg2[:, m, :]), pair_ps(0, m), ACT.Sigmoid).then_inc(S_("sg2_ready" if m == 0 else "mping_free"), 1)
                split_hi(6 * i + (UM + 6), 0, k=3 * i + (h0 + 3))
            for j in range(1, 9):
                split_hi(UO + j, j % 2, k=(UO + j) // 2)
            act.wait_ge(S_("o_free"), 2 + 4)
            squares(2)
            root(2)
            ffn(U2, C_FFN, 1)

        @block.vector
        def _(dve):
            own = [0]

            def link(ins):
                own[0] += 1
                ins.then_inc(S_("dve_own"), 1)
                return ins

            def settle():
                dve.wait_ge(S_("dve_own"), own[0])

            def lk(ins):
                link(ins)
                settle()

            def split_lo(u, slot, n=1024):
                dve.wait_ge(S_("hi_ready"), u + 1)
                dve.tensor_tensor(w_lo[:, slot, 0:n], w_raw[:, slot, 0:n], w_hi[:, slot, 0:n].bitcast(F32), ALU.subtract)\
                    .then_inc(S_("lo_ready"), 1)

            def norm(n, gain):
                dve.wait_ge(S_("sums_ready"), n + 1)
                dve.tensor_scalar(halves(rstd[:, :]), ps[:, 0:2, 0:HALF], 1.0 / D, EPS, ALU.mult, ALU.add).then_inc(S_("ms_ready"), 1)
                dve.wait_ge(S_("root_ready"), n + 1)
                lk(dve.reciprocal(rstd[:, :], rstd[:, :]))
                for k in range(KD):
                    t = hf[:, k % 2, :]
                    lk(dve.scalar_tensor_tensor(out=t, in0=xT[:, k, :], scalar=gain[:, k:k + 1], in1=rstd[:, :], op0=ALU.mult, op1=ALU.mult))
                    lk(dve.tensor_copy(h_hi[:, k, :], t))
                    dve.tensor_tensor(h_lo[:, k, :], t, h_hi[:, k, :].bitcast(F32), ALU.subtract).then_inc(S_("h_ready"), 1)
                dve.wait_ge(S_("h_ready"), KD * (n + 1))

            def ffn(u0, f):
                with dve.Fori(0, FF // 256) as i:
                    for j in range(1, 5):
                        split_lo(4 * i + (u0 + j), j % 2)
                    dve.wait_ge(S_("unit_used"), 4 * i + (u0 + 6))
                    dve.wait_ge(S_("ping_free"), i + (C_FFN * f + 2))
                    for m in range(2):
                        dve.tensor_tensor(halves(prod_t[:, m, :]), halves(silu_g[:, m, :]), pair_ps(1, m), ALU.mult).then_inc(S_("prod_taken"), 1)
                    dve.wait_ge(S_("prod_taken"), 2 * i + (22 * f + 3))
                    dve.sem_inc(S_("pong_free"), 1)
                    for m in range(2):
                        dve.tensor_copy(a_hi[:, bass.ds(2 * i + m, 1), :].rearrange("p o n -> p (o n)"), prod_t[:, m, :]).then_inc(S_("ahi_ready"), 1)
                    dve.wait_ge(S_("ahi_ready"), 2 * i + (22 * f + 2))
                    for m in range(2):
                        dve.tensor_tensor(a_lo[:, bass.ds(2 * i + m, 1), :].rearrange("p o n -> p (o n)"), prod_t[:, m, :],
                                          a_hi[:, bass.ds(2 * i + m, 1), :].rearrange("p o n -> p (o n)").bitcast(F32), ALU.subtract)\
                            .then_inc(S_("act_ready"), 1)
                    dve.wait_ge(S_("act_ready"), 2 * i + (22 * f + 2))
                for i in range(2):
                    for half in range(2):
                        for j in range(6 * half + 1, 6 * half + 7):
                            if f == 0 or i == 0 or j < 12:
                                split_lo(12 * i + (u0 + 44 + j), j % 2, n=512 if j % 6 == 5 else 1024)
                        dve.wait_ge(S_("unit_used"), 12 * i + (u0 + 44 + 6 * half + 5 + 3))
                        for m in range(2):
                            xm = halves(xT[:, 4 * i + 2 * half + m, :])
                            ins = dve.scalar_tensor_tensor(out=xm, in0=pair_ps(half, m), scalar=0.5, in1=xm, op0=ALU.mult, op1=ALU.add)
                            ins.then_inc(S_("x_updated" if m == 0 else ("ping_free" if half == 0 else "pong_free")), 1)

            dve.sem_inc(S_("lo_ready"), 2)
            dve.sem_inc(S_("unit_used"), 2)
            dve.sem_inc(S_("ping_free"), 1)
            dve.sem_inc(S_("pong_free"), 1)
            dve.sem_inc(S_("kv_used"), 4)
            dve.sem_inc(S_("pv_used"), 4)
            dve.sem_inc(S_("mping_free"), 1)
            dve.sem_inc(S_("mpong_free"), 1)
            dve.sem_inc(S_("o_free"), 2)
            for name in ("search", "prod_taken", "logits_ready", "mz_ready", "att_group", "m_ready"):
                dve.sem_inc(S_(name), 1)
            dve.memset(ones[:, :], 1.0).then_inc(S_("ones_ready"), 1)
            split_lo(0, 0)
            dve.wait_ge(S_("gain_in"), 16 * 14)
            dve.wait_ge(S_("xt_evac"), 2 * TB)
            norm(0, g1c)
            ffn(U1, 0)
            norm(1, gmc)

            dve.wait_ge(S_("rope_in"), 32)
            dve.wait_ge(S_("nat_evac"), TB)
            x = idxn[:, :, 0:288].rearrange("p b (h two d) -> p b h two d", two=2, d=16)
            ob = iro[:, :, 0:9, :].rearrange("p b h (two d) -> p b h two d", two=2)
            t1 = rt1[:, :, :, :].rearrange("p b h d -> p b (h d)")[:, :, 0:144].rearrange("p b (h d) -> p b h d", d=16)
            t2 = rt2[:, :, :, :].rearrange("p b h d -> p b (h d)")[:, :, 0:144].rearrange("p b (h d) -> p b h d", d=16)

            def rope(x1, x2, o1, o2, cos, sin, a, b):
                link(dve.tensor_tensor(a, x1, cos, ALU.mult))
                lk(dve.tensor_tensor(b, x2, sin, ALU.mult))
                lk(dve.tensor_tensor(a, a, b, ALU.subtract))
                link(dve.tensor_tensor(b, x1, sin, ALU.mult))
                lk(dve.tensor_tensor(x2, x2, cos, ALU.mult))
                link(dve.tensor_tensor(o2, b, x2, ALU.add))
                lk(dve.tensor_copy(o1, a))

            def bc(tab, c0, c1, nh):
                return tab[:, :, c0:c1].unsqueeze(2).to_broadcast([P, TB, nh, c1 - c0])

            rope(x[:, :, :, 0, :], x[:, :, :, 1, :], ob[:, :, :, 0, :], ob[:, :, :, 1, :],
                 bc(ropei, 0, 16, 9), bc(ropei, 16, 32, 9), t1, t2)
            link(dve.tensor_scalar(wisc[:, :, :], idxn[:, :, 288:296], IDX_SCALE, None, ALU.mult))
            dve.tensor_copy(iro[:, :, 9:12, :], iro[:, :, 8:9, :].to_broadcast([P, TB, 3, ID])).then_inc(S_("iro_ready"), 1)
            dve.wait_ge(S_("iro_ready"), 1)
            settle()
            dve.tensor_copy(qrep[:, :, :, :], iro[0:NS, 0, 0:8, :].unsqueeze(2).to_broadcast([NS, IH, 4, ID])).then_inc(S_("qrep_ready"), 1)
            msq = small[:, 8:8 + TB * H]
            for w, (src, g) in enumerate(((qn, gqb), (kn, gkb))):
                dve.wait_ge(S_("nat_evac"), TB * (w + 2))
                v = src[:, :, :].rearrange("p b (h d) -> p (b h) d", d=HD)
                wk = rt1[:, :, :, :].rearrange("p b h d -> p (b h) d")
                for hh in range(2):
                    lk(dve.tensor_tensor(wk, v[:, :, 32 * hh:32 * hh + 32], v[:, :, 32 * hh:32 * hh + 32], ALU.mult))
                    lk(dve.tensor_reduce(msq if hh == 0 else rt2[:, 0, 0:2, :].rearrange("p a b -> p (a b)")[:, 0:TB * H], wk, AX.X, ALU.add))
                lk(dve.tensor_tensor(msq, msq, rt2[:, 0, 0:2, :].rearrange("p a b -> p (a b)")[:, 0:TB * H], ALU.add))
                dve.tensor_scalar(msq, msq, 1.0 / HD, EPS, ALU.mult, ALU.add).then_inc(S_("qkms_ready"), 1)
                dve.wait_ge(S_("qkroot_ready"), w + 1)
                lk(dve.reciprocal(msq, msq))
                lk(dve.tensor_tensor(v, v, msq.unsqueeze(2).to_broadcast([P, TB * H, HD]), ALU.mult))
                lk(dve.tensor_tensor(v, v, g[:, :].unsqueeze(1).to_broadcast([P, TB * H, HD]), ALU.mult))
                v4 = src[:, :, :].rearrange("p b (h two d) -> p b h two d", two=2, d=32)
                rope(v4[:, :, :, 0, :], v4[:, :, :, 1, :], v4[:, :, :, 0, :], v4[:, :, :, 1, :],
                     bc(ropet, 0, 32, H), bc(ropet, 32, 64, H), rt1[:, :, :, :], rt2[:, :, :, :])
                dve.sem_inc(S_("qk_ready"), 1)
            dve.wait_ge(S_("nat_stored"), 1)
            dve.wait_ge(S_("qkT_evac"), 2 * TB)
            lk(dve.memset(qbd[:, :, :, :], 0.0))
            dve.wait_ge(S_("qrepT_done"), 1)
            for k4 in range(4):
                r = 32 * k4
                dst = qbd[r:r + 32, :, k4 // 2, 64 * (k4 % 2):64 * (k4 % 2) + 64].rearrange("p s (q h) -> p s q h", q=8)
                link(dve.tensor_copy(dst, ps[r:r + 32, 4, :].rearrange("p (h s q) -> p s q h", h=IH, s=NSEQ)))
            dve.wait_ge(S_("wv_in"), 32)
            dve.wait_ge(S_("spread_in"), 16)
            for s in range(NSEQ):
                link(dve.tensor_scalar(wst[:, s, :], spread[:, s, :], wv[:, s:s + 1], None, ALU.mult))
            settle()
            dve.sem_inc(S_("qbd_ready"), 1)
            dve.wait_ge(S_("scores_done"), 4 * NSEQ)
            for half in range(2):
                dst = S[64 * half:64 * half + 64, 0:PAST // 2].rearrange("p (g k f) -> p k g f", g=16, f=4)
                for pr in range(2):
                    for k2 in range(2):
                        link(dve.tensor_copy(dst[:, :, :, 2 * pr + k2],
                                             ps[64 * k2:64 * k2 + 64, 2 * half + pr, :].rearrange("p (k g) -> p k g", g=16)))
            link(dve.memset(S[0:64, PAST // 2:WIDTH], BARRED))
            dve.wait_ge(S_("newdots_done"), 1)
            dve.wait_ge(S_("mask_in"), 32)
            nr = relud[0:NS, 0, :].rearrange("p (h k) -> p h k", h=IH)
            lk(dve.scalar_tensor_tensor(out=nr, in0=ps[0:NS, 6, :].rearrange("p (h k) -> p h k", h=IH), scalar=0.0,
                                        in1=wisc[0:NS, 0, :].unsqueeze(2).to_broadcast([NS, IH, NS]), op0=ALU.max, op1=ALU.mult))
            lk(dve.tensor_reduce(relud[0:NS, 1, 0:NS], nr.rearrange("p h k -> p k h"), AX.X, ALU.add))
            lk(dve.tensor_tensor(relud[0:NS, 1, 64:64 + NS], relud[0:NS, 1, 0:NS], newmask[:, :], ALU.add))
            lk(dve.tensor_copy(S[64:128, PAST // 2:WIDTH], relud[0:NS, 1, 64:64 + NS]))
            dve.sem_inc(S_("S_ready"), 1)
            def u_part(pr, m):
                ch = 2 * pr + m
                a = pair_ps(0, m)
                sg = halves(sgb[:, m, :])
                link(dve.tensor_tensor(U_s[:, ch, :, CW - 1:CW - 1 + NEW], sgb[:, m, 0:NS].rearrange("p (s t) -> p s t", s=NSEQ),
                                       a[:, 0, 0:NS].rearrange("p (s t) -> p s t", s=NSEQ), ALU.mult))
                link(dve.tensor_tensor(U_p[:, ch, CW - 1:CW - 1 + HALF - NS], sg[:, 0, NS:HALF], a[:, 0, NS:HALF], ALU.mult))
                dve.tensor_tensor(U_p[:, ch, CW - 1 + HALF - NS:CW - 1 + SEQ], sg[:, 1, :], a[:, 1, :], ALU.mult).then_inc(S_("u_ready"), 1)

            link(dve.memset(U_p[:, :, 0:CW - 1], 0.0))
            for pr in range(2):
                dve.wait_ge(S_("sgb_ready"), 2 * pr + 2)
                for m in range(2):
                    u_part(pr, m)
            dve.wait_ge(S_("u_ready"), 4)
            settle()
            dve.tensor_copy(yacc[:, :, 0:NS].rearrange("p k (s t) -> p k s t", s=NSEQ), U_s[:, :, :, CW - 1:CW - 1 + NEW]).then_inc(S_("us_packed"), 1)
            dve.wait_ge(S_("unat_evac"), 1)
            dve.wait_ge(S_("us_state"), 2 * KC)
            ys = yacc[:, :, 0:NS].rearrange("p k (s t) -> p k s t", s=NSEQ)
            for j in range(CW):
                if j:
                    settle()
                for k in range(KC):
                    wj = wconv[:, k, j:j + 1]
                    if j == 0:
                        link(dve.tensor_scalar(yacc[:, k, NS:NT], U_p[:, k, 0:SEQ], wj, bconv[:, k:k + 1], ALU.mult, ALU.add))
                        link(dve.tensor_scalar(ys[:, k], U_s[:, k, :, 0:NEW], wj, bconv[:, k:k + 1], ALU.mult, ALU.add))
                    elif j < CW - 1:
                        link(dve.scalar_tensor_tensor(out=yacc[:, k, NS:NT], in0=U_p[:, k, j:j + SEQ], scalar=wj, in1=yacc[:, k, NS:NT], op0=ALU.mult, op1=ALU.add))
                        link(dve.scalar_tensor_tensor(out=ys[:, k], in0=U_s[:, k, :, j:j + NEW], scalar=wj, in1=ys[:, k], op0=ALU.mult, op1=ALU.add))
                    else:
                        link(dve.scalar_tensor_tensor(out=yacc[:, k, NS:NT], in0=U_p[:, k, j:j + SEQ], scalar=wj, in1=yacc[:, k, NS:NT], op0=ALU.mult, op1=ALU.add))
                        dve.scalar_tensor_tensor(out=ys[:, k], in0=U_s[:, k, :, j:j + NEW], scalar=wj, in1=ys[:, k], op0=ALU.mult, op1=ALU.add)\
                            .then_inc(S_("ln_in"), 1)
            dve.wait_ge(S_("ln_sums"), 1)
            mu = sgb[:, 0, :]
            lk(dve.tensor_scalar(halves(mu), ps[:, 4:6, 0:HALF], 1.0 / DC, None, ALU.mult))
            for k in range(KC):
                dve.tensor_tensor(yacc[:, k, :], yacc[:, k, :], mu, ALU.subtract).then_inc(S_("xc_ready"), 1)
            dve.wait_ge(S_("ln_sums"), 2)
            dve.tensor_scalar(halves(rstd[:, :]), ps[:, 6:8, 0:HALF], 1.0 / DC, EPS, ALU.mult, ALU.add).then_inc(S_("lnvar_ready"), 1)
            dve.wait_ge(S_("lnvar_ready"), 1)
            dve.wait_ge(S_("lnroot_ready"), 1)
            lk(dve.reciprocal(rstd[:, :], rstd[:, :]))
            for k in range(KC):
                dve.scalar_tensor_tensor(out=yacc[:, k, :], in0=yacc[:, k, :], scalar=gcln[:, k:k + 1], in1=rstd[:, :], op0=ALU.mult, op1=ALU.mult)\
                    .then_inc(S_("z_ready"), 1)
            for k in range(KC):
                dve.wait_ge(S_("swish_ready"), k + 1)
                lk(dve.tensor_copy(c_hi[:, k, :], yacc[:, k, :]))
                dve.tensor_tensor(c_lo[:, k, :], yacc[:, k, :], c_hi[:, k, :].bitcast(F32), ALU.subtract).then_inc(S_("c_ready"), 1)
            dve.wait_ge(S_("c_ready"), KC)

            flip, cur, x_, bit, okay, msb = (ismall[:, n:n + 1] for n in range(6))

            def count(thr, op, dst):
                return dve.tensor_scalar(EQ[:, :], S[:, :], thr, 0.0, op, ALU.add, accum_out=dst)

            link(dve.memset(flip, -1))
            link(dve.memset(cur, 0))
            link(dve.memset(bit, 1 << 30))
            link(dve.memset(msb, -(1 << 31)))
            count(0.0, ALU.is_ge, small[:, 0:1]).then_inc(S_("cnt_ready"), 1)
            settle()
            dve.wait_ge(S_("tot_ready"), 1)
            lk(dve.tensor_scalar(okay, ps[:, 7, 0:1], float(TOPK_S), None, ALU.is_ge))
            link(dve.copy_predicated(flip, okay, msb))
            lk(dve.copy_predicated(cur, okay, msb))
            with dve.Fori(0, 31) as i:
                dve.wait_ge(S_("search"), 4 * i + 1)
                dve.scalar_tensor_tensor(out=x_, in0=cur, scalar=bit, in1=flip, op0=ALU.bitwise_or, op1=ALU.bitwise_xor).then_inc(S_("search"), 1)
                dve.wait_ge(S_("search"), 4 * i + 2)
                count(x_.bitcast(F32), ALU.is_ge, small[:, 0:1]).then_inc(S_("cnt_ready"), 1)
                dve.wait_ge(S_("tot_ready"), i + 2)
                dve.tensor_scalar(okay, ps[:, 7, 0:1], float(TOPK_S), -1.0, ALU.is_ge, ALU.mult).then_inc(S_("search"), 1)
                dve.wait_ge(S_("search"), 4 * i + 3)
                dve.scalar_tensor_tensor(out=cur, in0=okay, scalar=bit, in1=cur, op0=ALU.bitwise_and, op1=ALU.bitwise_or).then_inc(S_("search"), 1)
                dve.wait_ge(S_("search"), 4 * i + 4)
                dve.tensor_scalar(bit, bit, 1, None, ALU.logical_shift_right).then_inc(S_("search"), 1)
            dve.wait_ge(S_("search"), 4 * 31 + 1)
            lk(dve.tensor_tensor(x_, cur, flip, ALU.bitwise_xor))
            thr = x_.bitcast(F32)
            lk(dve.tensor_scalar(SEL[:, :], S[:, :], thr, 0.0, ALU.is_gt, ALU.add, accum_out=small[:, 1:2]))
            count(thr, ALU.is_equal, small[:, 2:3]).then_inc(S_("cnt_ready"), 1)
            dve.wait_ge(S_("cnt_ready"), 33)
            link(dve.tensor_tensor_scan(CUM[:, :], EQ[:, :], EQ[:, :], 0.0, ALU.add, ALU.max))
            dve.wait_ge(S_("tot_ready"), 33)
            lk(dve.tensor_scalar(small[:, 3:4], ps[:, 7, 0:1], -1.0, float(TOPK_S), ALU.mult, ALU.add))
            lk(dve.scalar_tensor_tensor(out=EQ[:, :], in0=CUM[:, :], scalar=small[:, 3:4], in1=EQ[:, :], op0=ALU.is_le, op1=ALU.mult))
            dve.scalar_tensor_tensor(out=SEL[:, :], in0=SEL[:, :], scalar=1.0, in1=EQ[:, :], op0=ALU.mult, op1=ALU.add,
                                     accum_out=small[:, 4:5]).then_inc(S_("cnt_ready"), 1)
            dve.wait_ge(S_("tot_ready"), 34)
            dve.wait_ge(S_("cnt_ready"), 34)
            lk(dve.tensor_copy(small[:, 5:6], ps[:, 7, 0:1]))
            lk(dve.tensor_tensor_scan(CUM[:, :], SEL[:, :], SEL[:, :], small[:, 5:6], ALU.add, ALU.max))
            dve.tensor_tensor(CUM[:, :], CUM[:, :], SEL[:, :], ALU.mult).then_inc(S_("rank_ready"), 1)
            link(dve.tensor_scalar(nb[:, :], SEL[64:128, PAST // 2:WIDTH], -1.0, -OFF, ALU.add, ALU.mult))
            lk(dve.tensor_reduce(small[0:NS, 6:7], SEL[64:128, PAST // 2:WIDTH], AX.X, ALU.add))
            lk(dve.tensor_scalar(small[0:NS, 7:8], small[0:NS, 6:7], -1.0, float(TOPK_S), ALU.mult, ALU.add))
            link(dve.tensor_scalar(slotbias[:, :], slotno[:, :], small[0:NS, 7:8], OFF, ALU.is_ge, ALU.mult))
            for c4 in range(4):
                dve.wait_ge(S_("rankT_done"), c4 + 1)
                link(dve.tensor_scalar(RTi[:, 4 * c4:4 * c4 + 4, :], ps[:, c4, :].rearrange("p (c n) -> p c n", c=4), -1.0, None, ALU.add))
            settle()
            lk(dve.tensor_scalar(tmpi[:, :, :], RTi[:, :, :], 4, None, ALU.arith_shift_right))
            lk(dve.tensor_copy(adig[:, :, :], tmpi[:, :, :]))
            lk(dve.tensor_scalar(tmpi[:, :, :], RTi[:, :, :], 15, None, ALU.bitwise_and))
            lk(dve.tensor_copy(bdig[:, :, :], tmpi[:, :, :]))
            dve.wait_ge(S_("tab_in"), 16 * 4)
            link(dve.tensor_copy(digit[:, :, :], digitf[:, :, :]))
            link(dve.tensor_scalar(ptv[:, 1, :], ptb[:, :], 1, None, ALU.arith_shift_right))
            lk(dve.tensor_scalar(ptv[:, 0, :], ptb[:, :], 1, 7, ALU.bitwise_and, ALU.logical_shift_left))
            lk(dve.tensor_scalar(ptv[:, 0, :], ptv[:, 0, :], pcol[:, 0:1], None, ALU.add))
            for v in range(2):
                link(dve.tensor_copy(tab[:, v, :, :, :].rearrange("p s g q -> p (s g) q"),
                                     ptv[:, v, :].unsqueeze(2).to_broadcast([P, NSEQ * NPAGE, 8])))
            settle()

            def own_slots(s):
                dve.wait_ge(S_("slots_done"), s + 1)
                lk(dve.tensor_tensor(diag[:, :, :], ps[:, 5 + s % 2, 0:256].rearrange("p (x q) -> p x q", q=8), ownq[:, :, :], ALU.mult))
                lk(dve.tensor_reduce(rowidx[:, s, :], diag[:, :, :], AX.X, ALU.add))

            for s in range(NSEQ):
                if s:
                    dve.wait_ge(S_("slots_done"), s)
                for half in range(2):
                    pg = slice(16 * half, 16 * half + 16)
                    c0 = 64 * half + 8 * s
                    dg = digit[:, :, :].unsqueeze(1).to_broadcast([P, 16, 16, 8])
                    link(dve.tensor_tensor(ohA[:, pg, :, :], adig[:, :, c0:c0 + 8].unsqueeze(2).to_broadcast([P, 16, 16, 8]), dg, ALU.is_equal))
                    lk(dve.tensor_tensor(ohB[:, pg, :, :], bdig[:, :, c0:c0 + 8].unsqueeze(2).to_broadcast([P, 16, 16, 8]), dg, ALU.is_equal))
                    for v in range(2):
                        ins = dve.tensor_tensor(ohV[:, pg, v, :, :], ohB[:, pg, :, :], tab[:, v, s, pg, :].unsqueeze(2).to_broadcast([P, 16, 16, 8]), ALU.mult)
                        if half and v:
                            ins.then_inc(S_("onehot_ready"), 1)
                        else:
                            link(ins)
                if s:
                    own_slots(s - 1)
            own_slots(NSEQ - 1)
            dve.scalar_tensor_tensor(out=rowidx[:, :, 0:16], in0=rowidx[:, :, 16:32], scalar=256.0, in1=rowidx[:, :, 0:16],
                                     op0=ALU.mult, op1=ALU.add).then_inc(S_("rows_ready"), 1)
            dve.wait_ge(S_("idxT_done"), 1)
            dve.tensor_copy(idxT[:, :, :], ps[:, 6, 0:2 * NS].rearrange("p (c q) -> p c q", c=2)).then_inc(S_("idxT_ready"), 1)
            with dve.Fori(0, NS // 4) as i:
                for j in range(4):
                    dve.wait_ge(S_(f"kv_in{j}"), 32 * i + 32)
                    dve.wait_ge(S_(f"qb{j}"), 16 * i + 16)
                    dve.wait_ge(S_("logits_ready"), 4 * i + (j + 1))
                    dve.tensor_tensor(kprod[:, :, :], kv[:, j, :, :], qb[:, j, :].unsqueeze(1).to_broadcast([P, 2, DA]), ALU.mult)\
                        .then_inc(S_("kv_used"), 1)
                    dve.wait_ge(S_("kv_used"), 4 * i + (j + 5))
                    dve.tensor_reduce(G[:, :, bass.ds(4 * i + j, 1)].rearrange("p c o -> p (c o)"),
                                      kprod[:, :, :].rearrange("p c (h d) -> p (c h) d", h=H), AX.X, ALU.add).then_inc(S_("logits_ready"), 1)
            dve.wait_ge(S_("logitsT_done"), 1)
            link(dve.tensor_tensor(L[:, :, 0:TOPK_S], ps[0:NS, 0:4, :].rearrange("p b (h n) -> p (b h) n", h=2),
                                   slotbias[:, :].unsqueeze(1).to_broadcast([NS, H, TOPK_S]), ALU.add))
            lk(dve.tensor_tensor(L[:, :, TOPK_S:TOPK_S + NS], ps[0:NS, 4, :].rearrange("p (h n) -> p h n", h=H),
                                 nb[:, :].unsqueeze(1).to_broadcast([NS, H, NS]), ALU.add))
            mx, sm = small[0:NS, 8:16], small[0:NS, 16:24]
            lk(dve.tensor_reduce(mx, L[:, :, :], AX.X, ALU.max))
            dve.tensor_tensor(L[:, :, :], L[:, :, :], mx.unsqueeze(2).to_broadcast([NS, H, TOPK_S + NS]), ALU.subtract).then_inc(S_("shift_ready"), 1)
            dve.wait_ge(S_("exp_ready"), 1)
            lk(dve.tensor_reduce(sm, L[:, :, :], AX.X, ALU.add))
            lk(dve.reciprocal(sm, sm))
            dve.tensor_tensor(L[:, :, :], L[:, :, :], sm.unsqueeze(2).to_broadcast([NS, H, TOPK_S + NS]), ALU.mult).then_inc(S_("probs_ready"), 1)
            dve.wait_ge(S_("hm_in"), 32)
            with dve.Fori(0, 4) as g:
                dve.wait_ge(S_("pv_used"), 16 * g + 20)
                dve.wait_ge(S_("att_group"), g + 1)
                dve.tensor_tensor(mz[:, :], ps[:, 0, :], headmask[:, :], ALU.mult).then_inc(S_("mz_ready"), 1)
            dve.wait_ge(S_("att_group"), 5)
            lk(dve.tensor_copy(attT[:, :, 0:NS], ps[:, 4, 0:KA * NS].rearrange("p (k q) -> p k q", k=KA)))
            dve.tensor_tensor(attT[:, :, 0:NS], attT[:, :, 0:NS], ps[:, 5, 0:KA * NS].rearrange("p (k q) -> p k q", k=KA), ALU.add)\
                .then_inc(S_("atts_evac"), 1)
            link(dve.tensor_copy(biasp[:, 0, 0:P], causal[:, :]))
            n = 0
            for b in range(1, 4):
                nk = P * (b + 1)
                for h in range(IH):
                    dve.wait_ge(S_("prelu_ready"), n + 1)
                    w = wisc[:, b + 1, h:h + 1]
                    settle()
                    if n:
                        dve.wait_ge(S_("pscore_used"), n)
                    if h == 0:
                        dve.tensor_scalar(Sp[:, 0:nk], rp[:, n % 2, 0:nk], w, None, ALU.mult).then_inc(S_("pscore_used"), 1)
                    else:
                        dve.scalar_tensor_tensor(out=Sp[:, 0:nk], in0=rp[:, n % 2, 0:nk], scalar=w, in1=Sp[:, 0:nk], op0=ALU.mult, op1=ALU.add)\
                            .then_inc(S_("pscore_used"), 1)
                    n += 1
                dve.wait_ge(S_("pscore_used"), n)
                lk(dve.tensor_tensor(Sp[:, P * b:nk], Sp[:, P * b:nk], causal[:, :], ALU.add))
                for r in range(TOPK_P // 8):
                    lk(dve.max(m8[:, :], Sp[:, 0:nk]))
                    lk(dve.match_replace(Sp[:, 0:nk], m8[:, :], Sp[:, 0:nk], TAKEN))
                lk(dve.tensor_scalar(biasp[:, b, 0:nk], Sp[:, 0:nk], 2 * BARRED, OFF, ALU.is_ge, ALU.mult))
            def pmask(i):
                b = i // H
                nk = P * (b + 1)
                dve.wait_ge(S_("plog_done"), i + 1)
                if i >= 2:
                    dve.wait_ge(S_("pexp_ready"), i - 1)
                dve.tensor_tensor_reduce(Lp[:, i % 2, 0:nk], ps[:, i % 2, 0:nk], biasp[:, b, 0:nk], -HD ** -0.5, -TAKEN,
                                         ALU.add, ALU.min, small[:, 56 + i % 2:57 + i % 2]).then_inc(S_("plog_used"), 1)

            def pquot(i):
                b = i // H
                nk = P * (b + 1)
                dve.wait_ge(S_("pexp_ready"), i + 1)
                lk(dve.reciprocal(small[:, 60 + i % 2:61 + i % 2], small[:, 58 + i % 2:59 + i % 2]))
                dve.tensor_scalar(Pp[:, i % 2, 0:nk], Pp[:, i % 2, 0:nk], small[:, 60 + i % 2:61 + i % 2], None, ALU.mult)\
                    .then_inc(S_("pprob_ready"), 1)

            for i in range(33):
                if i < 32:
                    pmask(i)
                if i >= 1:
                    pquot(i - 1)
            split_lo(UM, 0)
            dve.wait_ge(S_("patt_evac"), 16)
            for k in range(KA):
                lk(dve.tensor_copy(t_hi[:, k, :], attT[:, k, :]))
                dve.tensor_tensor(t_lo[:, k, :], attT[:, k, :], t_hi[:, k, :].bitcast(F32), ALU.subtract).then_inc(S_("t_ready"), 1)
            with dve.Fori(0, 4) as i:
                for j in (1, 2, 3):
                    split_lo(6 * i + (UM + j), j % 2)
                dve.wait_ge(S_("unit_used"), 6 * i + (UM + 5))
                dve.wait_ge(S_("mping_free"), 2 * i + 2)
                for m in range(2):
                    dve.tensor_tensor(halves(mc[:, m, :]), halves(sg1[:, m, :]), pair_ps(1, m), ALU.mult)\
                        .then_inc(S_("mc_part" if m == 0 else "mpong_free"), 1)
                for j in (4, 5, 6):
                    split_lo(6 * i + (UM + j), j % 2)
                dve.wait_ge(S_("unit_used"), 6 * i + (UM + 8))
                dve.wait_ge(S_("mping_free"), 2 * i + 3)
                for m in range(2):
                    dve.tensor_tensor(halves(sg2[:, m, :]), halves(sg2[:, m, :]), pair_ps(1, m), ALU.mult)\
                        .then_inc(S_("mc_part" if m == 0 else "mpong_free"), 1)
                dve.wait_ge(S_("mpong_free"), 2 * i + 3)
                for m in range(2):
                    dve.tensor_tensor(mc[:, m, :], mc[:, m, :], sg2[:, m, :], ALU.add).then_inc(S_("merge_step"), 1)
                dve.wait_ge(S_("merge_step"), 4 * i + 2)
                mh = [m_hi[:, bass.ds(2 * i + m, 1), :].rearrange("p o n -> p (o n)") for m in range(2)]
                ml = [m_lo[:, bass.ds(2 * i + m, 1), :].rearrange("p o n -> p (o n)") for m in range(2)]
                for m in range(2):
                    dve.tensor_copy(mh[m], mc[:, m, :]).then_inc(S_("merge_step"), 1)
                dve.wait_ge(S_("merge_step"), 4 * i + 4)
                for m in range(2):
                    dve.tensor_tensor(ml[m], mc[:, m, :], mh[m].bitcast(F32), ALU.subtract).then_inc(S_("m_ready"), 1)
                dve.wait_ge(S_("m_ready"), 2 * i + 3)
            for pr in range(4):
                for j in (1, 2):
                    split_lo(UO + 2 * pr + j, j % 2)
                dve.wait_ge(S_("unit_used"), UO + 2 * pr + 4)
                for m in range(2):
                    xm = halves(xT[:, 2 * pr + m, :])
                    ins = dve.tensor_tensor(xm, xm, pair_ps(pr % 2, m), ALU.add)
                    ins.then_inc(S_("x_updated" if m == 0 else "o_free"), 1)
            norm(2, g2c)
            ffn(U2, 1)
            for f in range(2 * TB):
                n = NS if f < 2 else P
                dve.wait_ge(S_("y_done"), f + 1)
                dve.tensor_copy(xnat[0:n, f // 2, 512 * (f % 2):512 * (f % 2) + 512], ps[0:n, f % 2, :]).then_inc(S_("y_ready"), 1)

        @block.gpsimd
        def _(pool):
            def split_lo(u, slot, n):
                pool.wait_ge(S_("hi_ready"), u + 1)
                pool.tensor_tensor(w_lo[:, slot, 0:n], w_raw[:, slot, 0:n], w_hi[:, slot, 0:n].bitcast(F32), ALU.subtract)\
                    .then_inc(S_("lo_ready"), 1)

            pool.dma_start(out["conv_sample"][:, :, 0:CW - 1 - NEW, :], inp["state_conv"][:, :, NEW:CW - 1, :]).then_inc(S_("state_kept"), 16)
            pool.wait_ge(S_("ping_free"), C_FFN + 1)
            pool.wait_ge(S_("pong_free"), C_FFN + 1)
            pool.dma_start(ropet[:, :, :], con["rope"]).then_inc(S_("rope_in"), 16)
            pool.dma_start(ropei[:, :, :], con["ropei"]).then_inc(S_("rope_in"), 16)
            pool.wait_ge(S_("gain_in"), 16 * 14)
            ik_rows = inp["cache_idx_k"].rearrange("o n p d -> (o n) (p d)")
            pool.indirect_dma_start(ikn[:, :], None, ik_rows, bass.IndirectOffsetOnAxis(ap=ptile[:, 0:1], axis=0)).then_inc(S_("ik_in0"), 16)
            for name, dst, sem in (("pair", pairm, "sel_in"), ("first", firstm, "sel_in"), ("newmask", newmask, "mask_in"), ("slotno", slotno, "mask_in")):
                pool.dma_start(dst[:, :], con[name]).then_inc(S_(sem), 16)
            u = UA + 1
            for n in [2 * NI] * 3 + [2 * DA] * 12 + [1024]:
                split_lo(u, u % 2, n)
                u += 1
            pool.wait_ge(S_("iro_ready"), 1)
            pool.dma_start(wi_dram, wisc[0:NS, 0, :]).then_inc(S_("wi_saved"), 16)
            pool.wait_ge(S_("wi_saved"), 16)
            for k2 in range(2):
                pool.dma_start(wv[64 * k2:64 * k2 + 64, :], wi_dram.rearrange("(s q) h -> (q h) s", q=8), allow_slow_non_contiguous=True).then_inc(S_("wv_in"), 16)
            n_out = 0
            pool.wait_ge(S_("qk_ready"), 2)
            pool.wait_ge(S_("nat_evac"), 4 * TB)
            pool.dma_start(q_dram, qn[0:NS, 0, :]).then_inc(S_("q_saved"), 16)
            for tb in range(TB):
                n = NS if tb == 0 else P
                r0 = 0 if tb == 0 else P * (tb - 1)
                where = "sample" if tb == 0 else "prompt"
                for key, src in (("k_", kn[0:n, tb, :]), ("v_", vn[0:n, tb, :]), ("ik_", iro[0:n, tb, 8, :])):
                    pool.dma_start(out[key + where][r0:r0 + n], src).then_inc(S_("nat_out"), 16)
                    n_out += 1
            pool.wait_ge(S_("nat_out"), 16 * n_out)
            pool.wait_ge(S_("q_saved"), 16)
            pool.wait_ge(S_("qkT_evac"), 2 * TB)
            pool.wait_ge(S_("iT_evac"), TB)
            pool.wait_ge(S_("qrep_ready"), 1)
            pool.sem_inc(S_("nat_stored"), 1)
            pool.dma_start(spread[:, :, :], con["spread"]).then_inc(S_("spread_in"), 16)
            pool.dma_start(ptb[:, :], inp["page_table"].rearrange("(o s) n -> o (s n)", o=1).to_broadcast([P, NSEQ * NPAGE])).then_inc(S_("tab_in"), 16)
            pool.dma_start(digitf[:, :, :], con["digit"]).then_inc(S_("tab_in"), 16)
            pool.dma_start(pcol[:, :], con["pcol"]).then_inc(S_("tab_in"), 16)
            pool.dma_start(ownq[:, :, :], con["ownq"]).then_inc(S_("tab_in"), 16)
            pool.wait_ge(S_("ikT_evac"), 8)
            pool.indirect_dma_start(ikn[:, :], None, ik_rows, bass.IndirectOffsetOnAxis(ap=ptile[:, 1:2], axis=0)).then_inc(S_("ik_in1"), 16)
            pool.wait_ge(S_("S_ready"), 1)
            for b in range(2):
                pool.dma_start(stn[:, b, :], inp["state_conv"][0, 4 * b:4 * b + 4].rearrange("s t c -> (s t) c")).then_inc(S_("state_in"), 16)
            for u in range(UB + 1, UB + 8):
                split_lo(u, u % 2, 1024)
            pool.wait_ge(S_("unat_evac0"), 1)
            pool.dma_start(out["conv_prompt"], unat[P - (CW - 1):P, 0, :]).then_inc(S_("unat_out"), 16)
            pool.wait_ge(S_("unat_evac"), 1)
            pool.dma_start(out["conv_sample"][0, :, CW - 1 - NEW:CW - 1, :], unat[0:NS, 1, :]).then_inc(S_("unat_out"), 16)
            pool.wait_ge(S_("rows_ready"), 1)
            pool.dma_start(headmask[:, :], con["headmask"]).then_inc(S_("hm_in"), 16)
            pool.dma_start(qsel[:, :], con["qsel"]).then_inc(S_("hm_in"), 16)
            pool.dma_start(idx_dram.rearrange("a q s b -> (a q) s b"), rowidx[:, :, 0:16]).then_inc(S_("idx_saved"), 16)
            pool.wait_ge(S_("idx_saved"), 16)
            for s in range(NSEQ):
                pool.dma_start(idxr[8 * s:8 * s + 8, :].rearrange("q (a b) -> q a b", b=16), idx_dram[:, :, s, :].rearrange("a q b -> q a b"))\
                    .then_inc(S_("idx_back"), 16)
            pool.wait_ge(S_("idxT_ready"), 1)
            for w, name in enumerate(("cache_k", "cache_v")):
                rows = inp[name].rearrange("o n p h d -> (o n p) (h d)")
                if w == 1:
                    pool.wait_ge(S_("kv_used"), NS + 4)
                    pool.memset(zq[:, :, :, :], 0.0).then_inc(S_("zq_zero"), 1)
                with pool.Fori(0, NS // 4) as i:
                    for j in range(4):
                        pool.wait_ge(S_("pv_used" if w else "kv_used"), 4 * i + (j + 1))
                        pool.tensor_copy(slotidx[:, j, :], idxT[:, :, bass.ds(4 * i + j, 1)].rearrange("p c o -> p (c o)")).then_inc(S_("slot_set"), 1)
                        pool.wait_ge(S_("slot_set"), 4 * i + (NS * w + j + 1))
                        pool.sem_inc(S_("gather_turn"), 1)
                        for c in range(2):
                            pool.indirect_dma_start(kv[:, j, c, :], None, rows, bass.IndirectOffsetOnAxis(ap=slotidx[:, j, c:c + 1], axis=0))\
                                .then_inc(S_(f"kv_in{j}"), 16)
            pool.wait_ge(S_("state_kept"), 16)
            pool.wait_ge(S_("unat_out"), 32)


_IN = ["x_prompt", "x_sample", "cache_k", "cache_v", "cache_idx_k", "state_conv", "page_table", "g_ffn1", "w_ffn1_in",
       "w_ffn1_out", "g_mix", "w_in", "g_q", "g_k", "w_dw", "b_dw", "g_cln", "b_cln", "w_cout", "w_aout", "w_o",
       "g_ffn2", "w_ffn2_in", "w_ffn2_out"]
_OUT = [("y_prompt", (SEQ, D), (1, SEQ, D)), ("y_sample", (NS, D), (NSEQ, NEW, D)),
        ("k_prompt", (SEQ, DA), (1, 1, SEQ, H, HD)), ("v_prompt", (SEQ, DA), (1, 1, SEQ, H, HD)),
        ("ik_prompt", (SEQ, ID), (1, 1, SEQ, ID)), ("conv_prompt", (CW - 1, DC), (1, 1, CW - 1, DC)),
        ("k_sample", (NS, DA), (1, NSEQ, NEW, H, HD)), ("v_sample", (NS, DA), (1, NSEQ, NEW, H, HD)),
        ("ik_sample", (NS, ID), (1, NSEQ, NEW, ID)), ("conv_sample", (1, NSEQ, CW - 1, DC), (1, NSEQ, CW - 1, DC))]


def kernel(**inputs):
    import concourse.bacc as bacc
    from concourse.bass_utils import run_bass_kernel_spmd

    nc = bacc.Bacc("TRN2", target_bir_lowering=False, num_devices=1)
    arrays, inp, con, out = {}, {}, {}, {}
    for name in _IN:
        a = np.ascontiguousarray(inputs[name])
        if name in ("x_prompt", "x_sample"):
            a = a.reshape(-1, D)
        arrays[name] = a
        inp[name] = nc.dram_tensor(name, a.shape, mybir.dt.from_np(a.dtype), kind="ExternalInput").ap()
    for name, a in constants().items():
        arrays["c_" + name] = a
        con[name] = nc.dram_tensor("c_" + name, a.shape, F32, kind="ExternalInput").ap()
    for name, shape, _ in _OUT:
        out[name] = nc.dram_tensor("o_" + name, shape, F32, kind="ExternalOutput").ap()
    hybrid_step(nc, inp, con, out)
    r = run_bass_kernel_spmd(nc, [arrays], core_ids=[0])
    return tuple(r.results[0]["o_" + name].reshape(shape) for name, _, shape in _OUT)
```

```python
from contextlib import ExitStack

import numpy as np

import concourse.bass as bass
from concourse import mybir

ALU = mybir.AluOpType
ACT = mybir.ActivationFunctionType
AX = mybir.AxisListType
F32 = mybir.dt.float32
F32R = mybir.dt.float32r
BF16 = mybir.dt.bfloat16
I32 = mybir.dt.int32

P = 128
D = 1024
SEQ, NSEQ, NEW = 512, 8, 8
NS = NSEQ * NEW
NT = NS + SEQ
HALF = NT // 2
KD = D // P
FF = 2816
KF = FF // P
H, HD = 8, 64
DA = H * HD
KA = DA // P
IH, ID = 8, 32
CW = 31
DC = 512
KC = DC // P
PAGE, NPAGE, NPHYS = 128, 32, 320
PAST = PAGE * NPAGE
TOPK_S, TOPK_P = 256, 128
WIDTH = PAST // 2 + NS
TB = 5
EPS = 1e-6
IDX_SCALE = (IH * ID) ** -0.5
BARRED = -1e38
TAKEN = -3e38
OFF = -1e30
P_IN = 2 * DC + 3 * DA + IH * ID + ID + IH + 2 * D
COL_A, COL_B = 0, DC
COL_Q, COL_K, COL_V = 2 * DC, 2 * DC + DA, 2 * DC + 2 * DA
COL_I = 2 * DC + 3 * DA
NI = IH * ID + ID + IH
COL_GC = COL_I + NI
COL_GA = COL_GC + D


def block_cols(tb):
    return (0, P) if tb == 0 else (NS + P * (tb - 1), NS + P * tb)


def constants():
    c = {}
    p = np.arange(P)
    c["ident"] = np.eye(P, dtype=np.float32)
    pos = np.zeros((P, TB), np.float32)
    pos[:, 0] = np.where(p < NS, PAST + p % NEW, p - NS)
    for tb in range(1, TB):
        pos[:, tb] = P * (tb - 1) + p
    for name, d in (("rope", HD), ("ropei", ID)):
        half = d // 2
        inv = 10000.0 ** (-np.arange(half) * (2.0 / d))
        ang = (pos[:, :, None] * inv.astype(np.float32)[None, None, :]).astype(np.float32)
        c[name] = np.concatenate([np.cos(ang), np.sin(ang)], axis=-1).astype(np.float32)
    r_k4, r_q = p // 64, p % 64 // 8
    m = np.zeros((P, NSEQ, P), np.float32)
    for s in range(NSEQ):
        m[:, s, :] = (r_k4[:, None] == p[None, :] // 64) & (p[None, :] % 64 // 8 == s) & (r_q[:, None] == p[None, :] % 8)
    c["spread"] = m
    c["pair"] = (p[:, None] % 64 == p[None, :] % 64).astype(np.float32)
    c["first"] = ((p[:, None] < 64) & (p[None, :] == p[:, None] + 64)).astype(np.float32)
    t = np.arange(NS)
    c["newmask"] = np.where((t[:, None] // NEW == t[None, :] // NEW) & (t[None, :] <= t[:, None]), 0.0, BARRED).astype(np.float32)
    c["causal"] = np.where(p[None, :] <= p[:, None], 0.0, BARRED).astype(np.float32)
    c["digit"] = np.broadcast_to(np.arange(16, dtype=np.float32)[None, :, None], (P, 16, 8)).copy()
    c["slotno"] = np.broadcast_to(np.arange(TOPK_S, dtype=np.float32), (NS, TOPK_S)).copy()
    c["headmask"] = (p[:, None] % 8 == np.arange(DA)[None, :] // HD).astype(np.float32)
    c["qsel"] = (p[:, None] // 8 == np.arange(16)[None, :]).astype(np.float32)
    c["ownq"] = np.broadcast_to((p[:, None] % 8 == np.arange(8)[None, :])[:, None, :], (P, 32, 8)).astype(np.float32).copy()
    c["pcol"] = p[:, None].astype(np.float32)
    return c


def hybrid_step(nc, inp, con, out):
    ctx = ExitStack()
    with ctx:
        base0 = 16512
        used = {}

        def place(off, items):
            res = []
            for name, shape, dt in items:
                size = int(np.prod(shape[1:])) * (2 if dt == BF16 else 4)
                size = (size + 31) // 32 * 32
                assert off + size <= 229344, (name, off, size)
                res.append(nc.alloc_sbuf_tensor_at(name, list(shape), dt, offset=off))
                used[name] = (off, size)
                off += size
            return res, off

        (xT, h_hi, h_lo, w_raw, w_hi, w_lo, rstd, ident, ones, g1c, gmc, g2c, causal, ptile), arena = place(base0, [
            ("xT", (P, KD, NT), F32), ("h_hi", (P, KD, NT), F32R), ("h_lo", (P, KD, NT), F32R),
            ("w_raw", (P, 2, 1024), F32), ("w_hi", (P, 2, 1024), F32R), ("w_lo", (P, 2, 1024), F32R),
            ("rstd", (P, NT), F32), ("ident", (P, P), F32), ("ones", (P, P), F32),
            ("g1c", (P, KD), F32), ("gmc", (P, KD), F32), ("g2c", (P, KD), F32), ("causal", (P, P), F32),
            ("ptile", (P, 2), I32)])
        (small, ismall, wconv, bconv, gcln, bcln, gqb, gkb, slotbias, nb, slotidx, wv), arena = place(arena, [
            ("small", (P, 64), F32), ("ismall", (P, 8), I32), ("wconv", (P, KC, CW), F32), ("bconv", (P, KC), F32),
            ("gcln", (P, KC), F32), ("bcln", (P, KC), F32), ("gqb", (P, HD), F32), ("gkb", (P, HD), F32),
            ("slotbias", (NS, TOPK_S), F32), ("nb", (NS, NS), F32), ("slotidx", (P, 4, 2), I32), ("wv", (P, NSEQ), F32)])
        (a_hi, a_lo, silu_g, prod_t), _ = place(arena, [
            ("a_hi", (P, KF, NT), F32R), ("a_lo", (P, KF, NT), F32R), ("silu_g", (P, 2, NT), F32), ("prod_t", (P, 2, NT), F32)])
        (sq, hf, xnat), _ = place(arena, [("sq", (P, KD, NT), F32), ("hf", (P, 3, NT), F32), ("xnat", (P, TB, D), F32)])
        (vn, qT, kT, iT, wisc, S, attT, idxT), m1 = place(arena, [
            ("vn", (P, TB, DA), F32), ("qT", (P, KA, NT), F32), ("kT", (P, KA, NT), F32), ("iT", (P, 3, NT), F32),
            ("wisc", (P, TB, IH), F32), ("S", (P, WIDTH), F32), ("attT", (P, KA, NT), F32), ("idxT", (P, 2, NS), I32)])
        (U_p, U_s, sgb), _ = place(m1, [
            ("U_p", (P, KC, CW - 1 + SEQ), F32), ("U_s", (P, KC, NSEQ, CW - 1 + NEW), F32), ("sgb", (P, 2, NT), F32)])
        (gate_c,), m2 = place(m1, [("gate_c", (P, 4, 2, NT), F32)])
        (yacc, ysq), _ = place(used["h_hi"][0], [("yacc", (P, KC, NT), F32), ("ysq", (P, KC, NT), F32)])
        (c_hi, c_lo), _ = place(used["h_lo"][0], [("c_hi", (P, KC, NT), F32R), ("c_lo", (P, KC, NT), F32R)])
        (ikn,), _ = place(m1, [("ikn", (P, PAGE * ID), F32)])
        (idxn, iro, qn, kn, rt1, rt2), _ = place(m2, [
            ("idxn", (P, TB, NI), F32), ("iro", (P, TB, 12, ID), F32), ("qn", (P, TB, DA), F32), ("kn", (P, TB, DA), F32),
            ("rt1", (P, TB, H, 32), F32), ("rt2", (P, TB, H, 32), F32)])
        (qrep,), _ = place(used["S"][0], [("qrep", (NS, IH, 4, ID), F32)])
        (ikT, qbd, wst, spread, relud), _ = place(m2, [
            ("ikT", (P, 32, P), F32), ("qbd", (P, NSEQ, 2, P), F32), ("wst", (P, NSEQ, P), F32),
            ("spread", (P, NSEQ, P), F32), ("relud", (P, 2, 512), F32)])
        (EQ, CUM, SEL), _ = place(m2, [("EQ", (P, WIDTH), F32), ("CUM", (P, WIDTH), F32), ("SEL", (P, WIDTH), F32)])
        (pairm, firstm, newmask, slotno), lookups = place(used["attT"][0], [
            ("pairm", (P, P), F32), ("firstm", (P, P), F32), ("newmask", (NS, NS), F32), ("slotno", (NS, TOPK_S), F32)])
        (RTi,), _ = place(used["S"][0], [("RTi", (P, 16, P), I32)])
        (adig, bdig, ohA, ohB, ohV, tab, digit, ownq), _ = place(m2, [
            ("adig", (P, 16, P), BF16), ("bdig", (P, 16, P), BF16), ("ohA", (P, NPAGE, 16, 8), BF16),
            ("ohB", (P, NPAGE, 16, 8), BF16), ("ohV", (P, NPAGE, 2, 16, 8), BF16), ("tab", (P, 2, NSEQ, NPAGE, 8), BF16),
            ("digit", (P, 16, 8), BF16), ("ownq", (P, 32, 8), F32)])
        (tmpi,), _ = place(used["ohV"][0], [("tmpi", (P, 16, P), I32)])
        (ptb, diag, rowidx, idxr, digitf, pcol, ptv), e_ = place(lookups, [
            ("ptb", (P, NSEQ * NPAGE), I32), ("diag", (P, 32, 8), F32), ("rowidx", (P, NSEQ, 32), F32),
            ("idxr", (NS, TOPK_S), F32), ("digitf", (P, 16, 8), F32), ("pcol", (P, 1), F32), ("ptv", (P, 2, NSEQ * NPAGE), I32)])
        assert e_ <= used["attT"][0] + used["attT"][1]
        (kv, pT, pnT, zq, mz, G, qb, kprod), _ = place(m2, [
            ("kv", (P, 4, 2, DA), F32), ("pT", (P, 2, H, NS), F32), ("pnT", (NS, H, NS), F32),
            ("zq", (P, 4, 2, 248), F32), ("mz", (P, DA), F32), ("G", (P, 16, NS), F32), ("qb", (P, 4, DA), F32),
            ("kprod", (P, 2, DA), F32)])
        (conv_mean,), _ = place(used["sgb"][0], [("conv_mean", (P, NT), F32)])
        (gpack,), _ = place(used["sgb"][0], [("gpack", (P, KC, NS), F32)])
        (stn,), _ = place(used["kprod"][0] + used["kprod"][1], [("stn", (120, 2, DC), F32)])
        (unat,), _ = place(used["stn"][0], [("unat", (P, 2, DC), F32)])
        (L,), _ = place(used["qb"][0], [("L", (NS, H, TOPK_S + NS), F32)])
        (m8,), _ = place(used["S"][0] + used["qrep"][1], [("m8", (P, 8), F32)])
        (rp,), e_ = place(lookups + 1920, [("rp", (P, 2, SEQ), F32)])
        assert e_ <= used["attT"][0] + used["attT"][1]
        (bias_new,), _ = place(used["rt2"][0] + used["rt2"][1], [("bias_new", (P, 3, SEQ), F32)])
        (biasp, headmask, qsel, pTp), e_ = place(used["iT"][0], [
            ("biasp", (P, 3, SEQ), F32), ("headmask", (P, DA), F32), ("qsel", (P, 16), F32), ("pTp", (P, 2, 4, P), F32)])
        assert e_ <= used["attT"][0]
        (Lp, Pp), e_ = place(used["pT"][0], [("Lp", (P, 2, SEQ), F32), ("Pp", (P, 4, SEQ), F32)])
        assert e_ <= used["G"][0]
        (t_hi, t_lo), _ = place(used["vn"][0], [("t_hi", (P, KA, NT), F32R), ("t_lo", (P, KA, NT), F32R)])
        (m_hi, m_lo), _ = place(m2, [("m_hi", (P, KD, NT), F32R), ("m_lo", (P, KD, NT), F32R)])
        (mc, gate_a), _ = place(used["kT"][0], [("mc", (P, 2, NT), F32), ("gate_a", (P, 4, 2, NT), F32)])

        (ropet, ropei), _ = place(lookups, [("ropet", (P, TB, HD), F32), ("ropei", (P, TB, ID), F32)])

        ps = ctx.enter_context(nc.psum_tensor("ps", [P, 8, 512], F32))
        q_dram = nc.dram_tensor("q_scratch", (NS, DA), F32, kind="Internal").ap()
        wi_dram = nc.dram_tensor("wi_scratch", (NS, IH), F32, kind="Internal").ap()
        gate_dram = nc.dram_tensor("gate_scratch", (8, P, 2 * NT), F32, kind="Internal").ap()
        bias_dram = nc.dram_tensor("bias_scratch", (3, P, SEQ), F32, kind="Internal").ap()
        idx_dram = nc.dram_tensor("idx_scratch", (16, 8, NSEQ, 16), F32, kind="Internal").ap()

        sems = {}

        def S_(name):
            if name not in sems:
                sems[name] = ctx.enter_context(nc.semaphore(name))
            return sems[name]

        block = ctx.enter_context(nc.Block())

        U_FFN = KD // 4 * 2 * (FF // 256) + 4 * 6
        U1, UA = 0, U_FFN
        UB = UA + 16
        UG = UB + 8
        UM = UG + 16
        UO = UM + 8
        U2 = UO + 8
        C_FFN = 11 + 2

        def pair_ps(half, m):
            return ps[:, 4 * half + 2 * m:4 * half + 2 * m + 2, 0:HALF]

        def halves(ap):
            return ap.rearrange("p (h n) -> p h n", h=2)

        win_v = inp["w_in"].rearrange("o (k p) n -> p (o k) n", p=P)

        @block.sync
        def _(sp):
            def load(u, src, slot, n):
                sp.wait_ge(S_("lo_ready"), u + 1)
                sp.sem_inc(S_("load_turn"), 1)
                dst = w_raw[:, slot, 0:n]
                sp.dma_start(dst.rearrange("p (k n) -> p k n", k=src.shape[1]), src).then_inc(S_(f"raw{slot}"), 16)

            def ffn(u0, w1, w2):
                v1 = w1.rearrange("o (k p) n -> p (o k) n", p=P)
                v2 = w2.rearrange("o (k p) n -> p (o k) n", p=P)
                with sp.Fori(0, FF // 256) as i:
                    for j in range(4):
                        load(u0 + 4 * i + j, v1[:, 4 * (j % 2):4 * (j % 2) + 4, bass.ds(i * 256 + (j // 2) * FF, 256)], j % 2, 1024)
                with sp.Fori(0, 2) as i:
                    for j in range(12):
                        k0 = 4 * (j % 6)
                        k1 = min(k0 + 4, KF)
                        load(u0 + 44 + 12 * i + j, v2[:, k0:k1, bass.ds(i * 512 + (j // 6) * 256, 256)], j % 2, (k1 - k0) * 256)

            ffn(U1, inp["w_ffn1_in"], inp["w_ffn1_out"])
            u = UA
            for col, n in ((COL_I, NI), (COL_Q, DA), (COL_K, DA), (COL_V, DA)):
                for j in range(4):
                    load(u, win_v[:, 2 * j:2 * j + 2, col:col + n], u % 2, 2 * n)
                    u += 1
            for pr in range(2):
                for col in (COL_B, COL_A):
                    if pr == 0 and col == COL_A:
                        for b in range(3):
                            sp.wait_ge(S_("choice_ready"), b + 1)
                            sp.dma_start(bias_dram[b, :, 0:P * (b + 2)], bias_new[:, b, 0:P * (b + 2)]).then_inc(S_("choice_saved"), 16)
                        sp.wait_ge(S_("choice_saved"), 48)
                    for j in range(2):
                        load(u, win_v[:, 4 * j:4 * j + 4, col + 256 * pr:col + 256 * pr + 256], u % 2, 1024)
                        u += 1
            for col in (COL_GC, COL_GA):
                for i in range(4):
                    for j in range(2):
                        load(u, win_v[:, 4 * j:4 * j + 4, col + 256 * i:col + 256 * i + 256], j, 1024)
                        u += 1
            vc = inp["w_cout"].rearrange("o (k p) n -> p (o k) n", p=P)
            va = inp["w_aout"].rearrange("o (k p) n -> p (o k) n", p=P)
            load(UM, vc[:, :, 0:256], 0, 1024)
            load(UM + 1, va[:, :, 0:256], 1, 1024)
            sp.wait_ge(S_("rows_ready"), 1)
            for b in range(3):
                sp.dma_start(biasp[:, b, 0:P * (b + 2)], bias_dram[b, :, 0:P * (b + 2)]).then_inc(S_("choice_back"), 16)
            sp.wait_ge(S_("idxT_ready"), 1)
            with sp.Fori(0, NS // 4) as i:
                for j in range(4):
                    sp.wait_ge(S_("kv_used"), 4 * i + j + 1)
                    sp.dma_start(qb[:, j, :], q_dram[bass.ds(4 * i + j, 1), :].to_broadcast([P, DA])).then_inc(S_(f"qb{j}"), 16)
            with sp.Fori(0, 3) as i:
                load(2 * i + (UM + 2), vc[:, :, bass.ds(i * 256 + 256, 256)], 0, 1024)
                load(2 * i + (UM + 3), va[:, :, bass.ds(i * 256 + 256, 256)], 1, 1024)
            vo = inp["w_o"].rearrange("o (k p) n -> p (o k) n", p=P)
            with sp.Fori(0, 4) as i:
                for j in range(2):
                    load(UO + 2 * i + j, vo[:, 4 * j:4 * j + 4, bass.ds(i * 256, 256)], j, 1024)
            ffn(U2, inp["w_ffn2_in"], inp["w_ffn2_out"])
            for tb in range(TB):
                sp.wait_ge(S_("y_ready"), 2 * (tb + 1))
                dst = out["y_sample"] if tb == 0 else out["y_prompt"][P * (tb - 1):P * tb]
                sp.dma_start(dst, xnat[0:NS if tb == 0 else P, tb, :]).then_inc(S_("y_out"), 16)
            sp.wait_ge(S_("y_out"), 16 * TB)

        @block.tensor
        def _(pe):
            turns = [0]

            def turn(mm):
                turns[0] += 1
                mm.then_inc(S_("row_tile_done"), 1)
                pe.wait_ge(S_("row_tile_done"), turns[0])

            def unit(u, slot, x_hi, x_lo, kc0, nk, half, first, last, between=None):
                pe.wait_ge(S_("lo_ready"), u + 3)
                hi = w_hi[:, slot, 0:nk * 256].rearrange("p (k n) -> p k n", k=nk)
                lo = w_lo[:, slot, 0:nk * 256].rearrange("p (k n) -> p k n", k=nk)
                for m in range(2):
                    if m and between:
                        between()
                    for k in range(nk):
                        for w, x, fst in ((hi, x_hi, True), (hi, x_lo, False), (lo, x_hi, False)):
                            for hf_ in range(2):
                                mm = pe.matmul(ps[:, 4 * half + 2 * m + hf_, 0:HALF], w[:, k, m * P:(m + 1) * P],
                                               x[:, kc0 + k, hf_ * HALF:(hf_ + 1) * HALF],
                                               start=(first and k == 0 and fst), stop=(last and k == nk - 1 and w is lo))
                mm.then_inc(S_("unit_used"), 1)

            def norm_sums(n):
                for k in range(KD):
                    pe.wait_ge(S_("sq_ready"), KD * n + k + 1)
                    for hf_ in range(2):
                        mm = pe.matmul(ps[:, hf_, 0:HALF], ones[:, :], sq[:, k, hf_ * HALF:(hf_ + 1) * HALF],
                                       start=(k == 0), stop=(k == KD - 1))
                mm.then_inc(S_("sums_ready"), 1)

            def ffn(f, u0, ping0, pong0, hbase):
                pe.wait_ge(S_("h_ready"), hbase + 4)
                with pe.Fori(0, FF // 256) as i:
                    pe.wait_ge(S_("ping_free"), i + (ping0 + 1))
                    for j in range(4):
                        if j == 1:
                            pe.wait_ge(S_("h_ready"), hbase + KD)
                        if j == 2:
                            pe.wait_ge(S_("pong_free"), i + (pong0 + 1))
                        unit(4 * i + (u0 + j), j % 2, h_hi, h_lo, 4 * (j % 2), 4, j // 2, j % 2 == 0, j % 2 == 1)
                pe.wait_ge(S_("act_ready"), KF * (f + 1))
                with pe.Fori(0, 2) as i:
                    for j in range(12):
                        if j == 0:
                            pe.wait_ge(S_("ping_free"), i + (ping0 + 12))
                        if j == 6:
                            pe.wait_ge(S_("pong_free"), i + (pong0 + 12))
                        k0 = 4 * (j % 6)
                        unit(12 * i + (u0 + 44 + j), j % 2, a_hi, a_lo, k0, min(4, KF - k0), j // 6, j % 6 == 0, j % 6 == 5)

            pe.wait_ge(S_("const_in"), 16)
            for tb in range(TB):
                pe.wait_ge(S_(f"x_in{tb}"), 16)
                n = NS if tb == 0 else P
                for g in range(2):
                    f = 2 * tb + g
                    if f >= 2:
                        pe.wait_ge(S_("xt_evac"), f - 1)
                    for j in range(4):
                        mm = pe.transpose(ps[:, f % 2, j * n:(j + 1) * n], xnat[0:n, tb, (4 * g + j) * P:(4 * g + j + 1) * P],
                                          ident[0:n, 0:n])
                    mm.then_inc(S_("xt_done"), 1)
            pe.wait_ge(S_("ones_ready"), 1)
            norm_sums(0)
            ffn(0, U1, 0, 0, 0)
            norm_sums(1)
            def prompt_scores():
                pe.wait_ge(S_("iro_ready"), 1)
                for tb in range(TB):
                    n = NS if tb == 0 else P
                    if tb >= 2:
                        pe.wait_ge(S_("iT_evac"), tb - 1)
                    for j in range(3):
                        mm = pe.transpose(ps[:, 2 + tb % 2, j * n:(j + 1) * n], iro[0:n, tb, 4 * j:4 * j + 4, :].rearrange("p a b -> p (a b)"), ident[0:n, 0:n])
                    mm.then_inc(S_("iT_done"), 1)
                pe.wait_ge(S_("iT_evac"), TB)
                n = 0
                for b in range(1, 4):
                    nk = P * (b + 1)
                    for h in range(IH):
                        if n >= 2:
                            pe.wait_ge(S_("prelu_ready"), n - 1)
                        r = 32 * (h % 4)
                        pe.matmul(ps[:, 2 + n % 2, 0:nk], iT[r:r + 32, h // 4, NS + P * b:NS + P * (b + 1)], iT[r:r + 32, 2, NS:NS + nk],
                                  start=True, stop=True).then_inc(S_("pdots_done"), 1)
                        n += 1
                pe.wait_ge(S_("prelu_ready"), n)

            u = UA
            for g, n in enumerate((NI, DA, DA, DA)):
                if g == 2:
                    prompt_scores()
                for j in range(4):
                    if g == 0:
                        pe.wait_ge(S_("h_ready"), KD + 2 * j + 2)
                    pe.wait_ge(S_("lo_ready"), u + 3)
                    hi = w_hi[:, u % 2, 0:2 * n].rearrange("p (k n) -> p k n", k=2)
                    lo = w_lo[:, u % 2, 0:2 * n].rearrange("p (k n) -> p k n", k=2)
                    for tb in range(TB):
                        s = TB * g + tb
                        if j == 0 and s >= 8:
                            pe.wait_ge(S_("nat_evac"), s - 7)
                        c0, c1 = block_cols(tb)
                        for k in range(2):
                            kk = 2 * j + k
                            pe.matmul(ps[:, s % 8, 0:n], h_hi[:, kk, c0:c1], hi[:, k, :], start=(kk == 0), stop=False)
                            pe.matmul(ps[:, s % 8, 0:n], h_lo[:, kk, c0:c1], hi[:, k, :], start=False, stop=False)
                            mm = pe.matmul(ps[:, s % 8, 0:n], h_hi[:, kk, c0:c1], lo[:, k, :], start=False, stop=(kk == KD - 1))
                        if j == 3 and tb < TB - 1:
                            mm.then_inc(S_("nat_done"), 1)
                    mm.then_inc(S_("unit_used"), 1)
                    u += 1
            pe.wait_ge(S_("nat_evac"), 4 * TB)
            for w, src in enumerate((qn, kn)):
                pe.wait_ge(S_("qk_ready"), w + 1)
                for tb in range(TB):
                    n = NS if tb == 0 else P
                    f = TB * w + tb
                    if f >= 4:
                        pe.wait_ge(S_("qkT_evac"), f - 3)
                    for j in range(KA):
                        mm = pe.transpose(ps[:, f % 4, j * n:(j + 1) * n], src[0:n, tb, j * P:(j + 1) * P], ident[0:n, 0:n])
                    mm.then_inc(S_("qkT_done"), 1)
            pe.wait_ge(S_("qrep_ready"), 1)
            pe.wait_ge(S_("qkT_evac"), 2 * TB)
            for h in range(IH):
                mm = pe.transpose(ps[:, 4, h * NS:(h + 1) * NS], qrep[:, h, :, :].rearrange("p a b -> p (a b)"), ident[0:NS, 0:NS])
            mm.then_inc(S_("qrepT_done"), 1)
            n_tr = 0
            n_dot = 0

            def scores_w(i):
                s, hp = i // 4, i % 4
                pe.wait_ge(S_("relu_ready"), i + 1)
                mm = pe.matmul(ps[:, hp, :], wst[:, s, :], relud[:, i % 2, :], start=(s == 0), stop=(s == NSEQ - 1))
                mm.then_inc(S_("scores_done"), 1)

            for gseq in range(2):
                pe.wait_ge(S_(f"ik_in{gseq}"), 16)
                for f in range(8):
                    if n_tr >= 2:
                        pe.wait_ge(S_("ikT_evac"), n_tr - 1)
                    for j in range(4):
                        kg = 4 * f + j
                        mm = pe.transpose(ps[:, 6 + n_tr % 2, j * P:(j + 1) * P], ikn[:, kg * P:(kg + 1) * P], ident[:, :])
                    mm.then_inc(S_("ikT_done"), 1)
                    n_tr += 1
                pe.wait_ge(S_("ikT_evac"), n_tr)
                if gseq == 0:
                    pe.wait_ge(S_("qbd_ready"), 1)
                for s4 in range(4):
                    for hp in range(4):
                        s = 4 * gseq + s4
                        if n_dot >= 2:
                            pe.wait_ge(S_("relu_ready"), n_dot - 1)
                        c0 = s4 * 32 + (hp // 2) * 16
                        pe.matmul(ps[:, 4 + n_dot % 2, :], qbd[:, s, hp % 2, :], ikT[:, :, c0:c0 + 16], start=True, stop=True)\
                            .then_inc(S_("dots_done"), 1)
                        if n_dot >= 1:
                            scores_w(n_dot - 1)
                        n_dot += 1
            scores_w(n_dot - 1)
            pe.wait_ge(S_("relu_ready"), n_dot)
            for r in range(0, P, 32):
                for h in (r // 32, r // 32 + 4):
                    mm = pe.matmul(ps[0:NS, 6, h * NS:(h + 1) * NS], iT[r:r + 32, h // 4, 0:NS], iT[r:r + 32, 2, 0:NS], start=(h == 0), stop=True,
                                   skip_group_check=True)
                if r < 96:
                    turn(mm)
            mm.then_inc(S_("newdots_done"), 1)
            pe.wait_ge(S_("sel_in"), 16 * 2)
            pe.wait_ge(S_("cnt_ready"), 1)
            pe.matmul(ps[:, 7, 0:1], pairm[:, :], small[:, 0:1], start=True, stop=True).then_inc(S_("tot_ready"), 1)
            def total(n):
                pe.wait_ge(S_("cnt_ready"), n)
                pe.matmul(ps[:, 7, 0:1], pairm[:, :], small[:, 0:1], start=True, stop=True).then_inc(S_("tot_ready"), 1)

            with pe.Fori(0, 7) as i:
                pe.wait_ge(S_("mix_free"), i + 1)
                for j in range(2):
                    unit(2 * i + (UB + j), j, h_hi, h_lo, 4 * j, 4, 0, j == 0, j == 1, between=(lambda: total(4 * i + (2 * j + 2))))
                    total(4 * i + (2 * j + 3))
            for n in range(28, 31):
                total(n + 2)
            pe.wait_ge(S_("cnt_ready"), 33)
            pe.matmul(ps[:, 7, 0:1], pairm[:, :], small[:, 1:2], start=True, stop=False)
            pe.matmul(ps[:, 7, 0:1], firstm[:, :], small[:, 2:3], start=False, stop=True).then_inc(S_("tot_ready"), 1)
            pe.wait_ge(S_("cnt_ready"), 34)
            pe.matmul(ps[:, 7, 0:1], firstm[:, :], small[:, 4:5], start=True, stop=True).then_inc(S_("tot_ready"), 1)
            pe.wait_ge(S_("rank_ready"), 1)
            pe.wait_ge(S_("mix_free"), 8)
            for c in range(16):
                mm = pe.transpose(ps[:, c // 4, (c % 4) * P:(c % 4 + 1) * P], CUM[:, c * P:(c + 1) * P], ident[:, :])
                if c % 4 == 3:
                    mm.then_inc(S_("rankT_done"), 1)
            def gate_unit(n):
                if n == 0:
                    pe.wait_ge(S_("ranks_taken"), 1)
                if n % 2 == 0:
                    pe.wait_ge(S_("mix_free"), 8 + n // 2)
                unit(UG + 6 + n, n % 2, h_hi, h_lo, 4 * (n % 2), 4, 0, n % 2 == 0, n % 2 == 1)

            for s in range(NSEQ):
                for pg in range(NPAGE):
                    if pg % 16 == 0:
                        pe.wait_ge(S_("onehot_ready"), 2 * s + pg // 16 + 1)
                    mm = pe.matmul(ps[:, 5 + s % 2, 0:256], ohA[:, pg, :, :].rearrange("p a b -> p (a b)"),
                                   ohV[:, pg, :, :, :].rearrange("p v a b -> p (v a b)"), start=(pg == 0), stop=(pg == NPAGE - 1))
                    if pg % 16 == 15:
                        mm.then_inc(S_("onehot_used"), 1)
                gate_unit(s)
            gate_unit(NSEQ)
            gate_unit(NSEQ + 1)
            pe.wait_ge(S_("idx_back"), 16 * NSEQ)
            for c in range(2):
                mm = pe.transpose(ps[:, 6, c * NS:(c + 1) * NS], idxr[:, c * P:(c + 1) * P], ident[0:NS, 0:NS])
            mm.then_inc(S_("idxT_done"), 1)
            for r in (0, 64):
                for h in range(r // 64, H, 2):
                    mm = pe.matmul(ps[0:NS, 4, h * NS:(h + 1) * NS], qT[r:r + 64, h // 2, 0:NS], kT[r:r + 64, h // 2, 0:NS], start=(h == 0), stop=True,
                                   skip_group_check=True)
                turn(mm)
            pe.wait_ge(S_("mix_free"), 13)
            pe.wait_ge(S_("state_in"), 16 * 2)
            for b in range(2):
                for j in range(KC):
                    mm = pe.transpose(ps[:, b, j * 120:(j + 1) * 120], stn[:, b, j * P:(j + 1) * P], ident[0:120, 0:120])
                mm.then_inc(S_("st_done"), 1)
            for j in range(KC):
                pe.transpose(ps[0:P, 2, j * P:(j + 1) * P], U_p[:, j, CW - 1 + SEQ - P:CW - 1 + SEQ], ident[:, :])
            pe.wait_ge(S_("us_packed"), 1)
            for j in range(KC):
                mm = pe.transpose(ps[0:NS, 3, j * P:(j + 1) * P], gpack[:, j, :], ident[:, :])
            mm.then_inc(S_("unat_done"), 1)
            pe.wait_ge(S_("unat_evac"), 1)
            steps = [(b, h) for b in range(4) for h in range(H)]

            def plogits(i):
                b, h = steps[i]
                r = 64 * (h % 2)
                if i >= 2:
                    pe.wait_ge(S_("plog_used"), i - 1)
                pe.matmul(ps[:, i % 2, 0:P * (b + 1)], qT[r:r + 64, h // 2, NS + P * b:NS + P * (b + 1)], kT[r:r + 64, h // 2, NS:NS + P * (b + 1)],
                          start=True, stop=True).then_inc(S_("plog_done"), 1)

            def pturn(i):
                b, h = steps[i]
                pe.wait_ge(S_("pprob_ready"), i + 1)
                if i >= 2:
                    pe.wait_ge(S_("pturn_evac"), i - 1)
                for kb in range(b + 1):
                    mm = pe.transpose(ps[:, 2 + i % 2, kb * P:(kb + 1) * P], Pp[:, i % 4, kb * P:(kb + 1) * P], ident[:, :])
                mm.then_inc(S_("pturn_done"), 1)

            def pvalue(i):
                b, h = steps[i]
                r = 64 * (h % 2)
                pe.wait_ge(S_("pturn_evac"), i + 1)
                if i >= 4:
                    pe.wait_ge(S_("patt_evac"), i // 2 - 1)
                for kb in range(b + 1):
                    mm = pe.matmul(ps[r:r + 64, 6 + i // 2 % 2, 0:P], vn[:, kb + 1, h * HD:(h + 1) * HD], pTp[:, i % 2, kb, :],
                                   start=(kb == 0), stop=(kb == b))
                mm.then_inc(S_("patt_done"), 1)

            for i in range(len(steps) + 3):
                if i < len(steps):
                    plogits(i)
                if 2 <= i <= len(steps) + 1:
                    pturn(i - 2)
                if i >= 3:
                    pvalue(i - 3)
            pe.wait_ge(S_("patt_evac"), 16)
            pe.wait_ge(S_("logits_ready"), NS + 1)
            for h in range(H):
                for c in range(2):
                    mm = pe.transpose(ps[0:NS, h // 2, (h % 2) * 256 + c * P:(h % 2) * 256 + (c + 1) * P], G[:, c * H + h, :], ident[:, :])
            mm.then_inc(S_("logitsT_done"), 1)
            pe.wait_ge(S_("probs_ready"), 1)
            for c in range(2):
                for h in range(H):
                    pe.transpose(ps[:, 5 + c, h * NS:(h + 1) * NS], L[:, h, c * P:(c + 1) * P], ident[0:NS, 0:NS])
            for h in range(H):
                mm = pe.transpose(ps[0:NS, 7, h * NS:(h + 1) * NS], L[:, h, TOPK_S:TOPK_S + NS], ident[0:NS, 0:NS])
            mm.then_inc(S_("probsT_done"), 1)
            pe.wait_ge(S_("probsT_evac"), 2)
            for h in range(H):
                r = 64 * (h % 2)
                mm = pe.matmul(ps[r:r + 64, 5, (h // 2) * NS:(h // 2 + 1) * NS], vn[0:NS, 0, h * HD:(h + 1) * HD], pnT[:, h, :],
                               start=(h < 2), stop=True, skip_group_check=True)
            with pe.Fori(0, 4) as g:
                for qi in range(16):
                    j = qi % 4
                    pe.wait_ge(S_(f"kv_in{j}"), 32 * (16 + 4 * g + qi // 4 + 1))
                    pe.wait_ge(S_("zq_ready"), 16 * g + (qi + 1))
                    if qi == 0:
                        pe.wait_ge(S_("mz_ready"), g + 1)
                    for c in range(2):
                        mm = pe.matmul(ps[:, 0, :], zq[:, j, c, 120 - 8 * qi:248 - 8 * qi], kv[:, j, c, :],
                                       start=(qi == 0 and c == 0), stop=(qi == 15 and c == 1))
                    mm.then_inc(S_("pv_used"), 1)
                pe.wait_ge(S_("mz_ready"), g + 2)
                for hp in range(KA):
                    mm = pe.matmul(ps[:, 4, bass.ds(16 * g + hp * NS, 16)], mz[:, hp * P:(hp + 1) * P], qsel[:, :],
                                   start=True, stop=True, skip_group_check=True)
                mm.then_inc(S_("att_group"), 1)
            for st in range(2):
                for k in range(KC):
                    pe.wait_ge(S_("ln_in"), KC * st + k + 1)
                    for hf_ in range(2):
                        mm = pe.matmul(ps[:, (1, 6)[st] + hf_, 0:HALF], ones[:, :], (ysq if st else yacc)[:, k, hf_ * HALF:(hf_ + 1) * HALF],
                                       start=(k == 0), stop=(k == KC - 1))
                mm.then_inc(S_("ln_sums"), 1)
            pe.wait_ge(S_("atts_evac"), 1)
            pe.wait_ge(S_("c_ready"), KC)
            pe.wait_ge(S_("t_ready"), KA)
            with pe.Fori(0, 4) as i:
                pe.wait_ge(S_("merge_free"), 2 * i + 1)
                unit(2 * i + UM, 0, c_hi, c_lo, 0, 4, 0, True, True)
                pe.wait_ge(S_("merge_free"), 2 * i + 2)
                unit(2 * i + (UM + 1), 1, t_hi, t_lo, 0, 4, 1, True, True)
            pe.wait_ge(S_("m_ready"), KD + 1)
            with pe.Fori(0, 2) as i:
                for half in range(2):
                    pe.wait_ge(S_("o_free"), 2 * i + (half + 1))
                    unit(4 * i + (UO + 2 * half), 0, m_hi, m_lo, 0, 4, half, True, False)
                    unit(4 * i + (UO + 2 * half + 1), 1, m_hi, m_lo, 4, 4, half, False, True)
            norm_sums(2)
            ffn(1, U2, C_FFN, C_FFN, 2 * KD)
            pe.wait_ge(S_("pong_free"), 2 * C_FFN + 1)
            for tb in range(TB):
                n = NS if tb == 0 else P
                c0 = 0 if tb == 0 else NS + P * (tb - 1)
                for g in range(2):
                    f = 2 * tb + g
                    if f >= 2:
                        pe.wait_ge(S_("y_ready"), f - 1)
                    for j in range(4):
                        mm = pe.transpose(ps[0:n, f % 2, j * P:(j + 1) * P], xT[:, 4 * g + j, c0:c0 + n], ident[:, :])
                    mm.then_inc(S_("y_done"), 1)

        @block.scalar
        def _(act):
            own = [0]

            def link(ins):
                own[0] += 1
                ins.then_inc(S_("act_own"), 1)

            def settle():
                act.wait_ge(S_("act_own"), own[0])

            def split_hi(u, slot, n=1024, k=None):
                act.wait_ge(S_(f"raw{slot}"), 16 * (k + 1))
                act.wait_ge(S_("unit_used"), u + 1)
                act.activation(w_hi[:, slot, 0:n], w_raw[:, slot, 0:n], ACT.Copy).then_inc(S_("hi_ready"), 1)

            def squares(n):
                for k in range(KD):
                    act.activation(sq[:, k, :], xT[:, k, :], ACT.Square).then_inc(S_("sq_ready"), 1)

            def root(n):
                act.wait_ge(S_("ms_ready"), n + 1)
                act.activation(rstd[:, :], rstd[:, :], ACT.Sqrt).then_inc(S_("root_ready"), 1)
                for k in range(KD):
                    act.wait_ge(S_("hf_ready"), KD * n + k + 1)
                    act.activation(h_hi[:, k, :], hf[:, k % 3, :], ACT.Copy).then_inc(S_("hhi_ready"), 1)

            def ffn(u0, ping0, f):
                with act.Fori(0, FF // 256) as i:
                    h0 = u0 // 2
                    split_hi(4 * i + (u0 + 1), 1, k=2 * i + h0)
                    split_hi(4 * i + (u0 + 2), 0, k=2 * i + (h0 + 1))
                    act.wait_ge(S_("unit_used"), 4 * i + (u0 + 4))
                    act.wait_ge(S_("prod_taken"), 2 * i + (22 * f + 1))
                    for m in range(2):
                        ins = act.activation(halves(silu_g[:, m, :]), pair_ps(0, m), ACT.Silu)
                        ins.then_inc(S_("silu_ready" if m == 0 else "ping_free"), 1)
                    split_hi(4 * i + (u0 + 3), 1, k=2 * i + (h0 + 1))
                    split_hi(4 * i + (u0 + 4), 0, k=2 * i + (h0 + 2))
                for i in range(2):
                    h0 = u0 // 2 + 22
                    for j in range(1, 13):
                        if f == 0 or i == 0 or j < 12:
                            split_hi(12 * i + (u0 + 44 + j), j % 2, n=512 if j % 6 == 5 else 1024, k=6 * i + (h0 + j // 2))

            act.dma_start(ident[:, :], con["ident"]).then_inc(S_("const_in"), 16)
            for tb in range(TB):
                n = NS if tb == 0 else P
                src = inp["x_sample"] if tb == 0 else inp["x_prompt"][P * (tb - 1):P * tb]
                act.dma_start(xnat[0:n, tb, :], src).then_inc(S_(f"x_in{tb}"), 16)
            for dst, name in ((g1c, "g_ffn1"), (gmc, "g_mix"), (g2c, "g_ffn2")):
                act.dma_start(dst[:, :], inp[name].rearrange("o (k p) -> p (o k)", p=P), allow_slow_non_contiguous=True).then_inc(S_("gain_in"), 16)
            act.dma_start(causal[:, :], con["causal"]).then_inc(S_("gain_in"), 16)
            for k in range(KC):
                act.dma_start(wconv[:, k, :], inp["w_dw"][0, :, k * P:(k + 1) * P].rearrange("w p -> p w"), allow_slow_non_contiguous=True)\
                    .then_inc(S_("gain_in"), 16)
            for dst, name in ((bconv, "b_dw"), (gcln, "g_cln"), (bcln, "b_cln")):
                act.dma_start(dst[:, :], inp[name].rearrange("o (k p) -> p (o k)", p=P), allow_slow_non_contiguous=True).then_inc(S_("gain_in"), 16)
            for dst, name in ((gqb, "g_q"), (gkb, "g_k")):
                act.dma_start(dst[:, :], inp[name].to_broadcast([P, HD])).then_inc(S_("gain_in"), 16)
            act.dma_start(ptile[:, :], inp["page_table"].rearrange("(g s) n -> (s n) g", g=2), allow_slow_non_contiguous=True).then_inc(S_("gain_in"), 16)
            split_hi(0, 0, k=0)
            for f in range(2 * TB):
                tb, g = f // 2, f % 2
                n = NS if tb == 0 else P
                c0 = 0 if tb == 0 else NS + P * (tb - 1)
                act.wait_ge(S_("xt_done"), f + 1)
                act.activation(xT[:, 4 * g:4 * g + 4, c0:c0 + n], ps[:, f % 2, 0:4 * n].rearrange("p (j n) -> p j n", j=4), ACT.Copy)\
                    .then_inc(S_("xt_evac"), 1)
            act.wait_ge(S_("xt_evac"), 2 * TB)
            squares(0)
            root(0)
            ffn(U1, 0, 0)
            act.wait_ge(S_("ping_free"), C_FFN + 1)
            act.wait_ge(S_("pong_free"), C_FFN + 1)
            squares(1)
            root(1)
            def prompt_scores():
                for tb in range(TB):
                    n = NS if tb == 0 else P
                    c0 = 0 if tb == 0 else NS + P * (tb - 1)
                    act.wait_ge(S_("iT_done"), tb + 1)
                    act.activation(iT[:, :, c0:c0 + n], ps[:, 2 + tb % 2, 0:3 * n].rearrange("p (j n) -> p j n", j=3), ACT.Copy)\
                        .then_inc(S_("iT_evac"), 1)
                for t in range(24):
                    b = 1 + t // 8
                    nk = P * (b + 1)
                    act.wait_ge(S_("pdots_done"), t + 1)
                    if t >= 2:
                        act.wait_ge(S_("pscore_used"), t - 1)
                    act.activation(rp[:, t % 2, 0:nk], ps[:, 2 + t % 2, 0:nk], ACT.Relu).then_inc(S_("prelu_ready"), 1)

            u = UA
            for g, (dst, n) in enumerate(((idxn, NI), (qn, DA), (kn, DA), (vn, DA))):
                if g == 2:
                    prompt_scores()
                for j in range(1, 5):
                    size = 2 * n if j < 4 else (2 * DA if g < 3 else 1024)
                    split_hi(u + j, (u + j) % 2, n=size, k=(u + j) // 2)
                for tb in range(TB):
                    if tb < TB - 1:
                        act.wait_ge(S_("nat_done"), 4 * g + tb + 1)
                    else:
                        act.wait_ge(S_("unit_used"), u + 6)
                    act.activation(dst[:, tb, :], ps[:, (TB * g + tb) % 8, 0:n], ACT.Copy).then_inc(S_("nat_evac"), 1)
                u += 4
            for w in range(2):
                act.wait_ge(S_("qkms_ready"), w + 1)
                act.activation(small[:, 8:8 + TB * H], small[:, 8:8 + TB * H], ACT.Sqrt).then_inc(S_("qkroot_ready"), 1)
            for f in range(2 * TB):
                w, tb = f // TB, f % TB
                n = NS if tb == 0 else P
                c0 = 0 if tb == 0 else NS + P * (tb - 1)
                act.wait_ge(S_("qkT_done"), f + 1)
                act.activation((kT if w else qT)[:, :, c0:c0 + n], ps[:, f % 4, 0:4 * n].rearrange("p (j n) -> p j n", j=4), ACT.Copy)\
                    .then_inc(S_("qkT_evac"), 1)
            nt, nd = 0, 0
            for gseq in range(2):
                if gseq == 1:
                    act.wait_ge(S_("dots_done"), 16)
                for f in range(8):
                    act.wait_ge(S_("ikT_done"), nt + 1)
                    if nt == 0:
                        act.wait_ge(S_("nat_stored"), 1)
                    act.activation(ikT[:, 4 * f:4 * f + 4, :], ps[:, 6 + nt % 2, :].rearrange("p (a n) -> p a n", a=4), ACT.Copy)\
                        .then_inc(S_("ikT_evac"), 1)
                    nt += 1
                for i in range(16):
                    act.wait_ge(S_("dots_done"), nd + 1)
                    if nd >= 2:
                        act.wait_ge(S_("scores_done"), nd - 1)
                    act.activation(relud[:, nd % 2, :], ps[:, 4 + nd % 2, :], ACT.Relu).then_inc(S_("relu_ready"), 1)
                    nd += 1
            h0 = UB // 2
            for pr in range(2):
                for j in range(1, 5):
                    split_hi(UB + 4 * pr + j, j % 2, k=h0 + 2 * pr + j // 2)
                    if j == 2:
                        act.wait_ge(S_("unit_used"), UB + 4 * pr + 4)
                        if pr == 1:
                            act.wait_ge(S_("u_ready"), 2)
                        for m in range(2):
                            act.activation(halves(sgb[:, m, :]), pair_ps(0, m), ACT.Sigmoid).then_inc(S_("sgb_ready" if m == 0 else "mix_free"), 1)
            act.wait_ge(S_("u_ready"), 4)
            h0 = UG // 2
            with act.Fori(0, 8) as i:
                split_hi(2 * i + (UG + 1), 1, k=i + h0)
                split_hi(2 * i + (UG + 2), 0, k=i + (h0 + 1))
                act.wait_ge(S_("unit_used"), 2 * i + (UG + 4))
                act.wait_ge(S_("gate_saved"), 16 * i + 16)
                for m in range(2):
                    act.activation(halves(sgb[:, m, :]), pair_ps(0, m), ACT.Sigmoid).then_inc(S_("gate_ready" if m == 0 else "mix_free"), 1)
                act.wait_ge(S_("gate_ready"), i + 1)
                act.wait_ge(S_("mix_free"), i + 6)
                act.sem_inc(S_("store_turn"), 1)
                act.dma_start(gate_dram[bass.ds(i, 1), :, :].rearrange("o p n -> p (o n)"), sgb[:, :, :].rearrange("p m n -> p (m n)"))\
                    .then_inc(S_("gate_saved"), 16)
            act.wait_ge(S_("gate_saved"), 16 * 9)
            act.activation(gpack[:, :, :].rearrange("p k (s t) -> p k s t", s=NSEQ), U_s[:, :, :, CW - 1:CW - 1 + NEW], ACT.Copy).then_inc(S_("us_packed"), 1)
            for b in range(2):
                act.wait_ge(S_("st_done"), b + 1)
                for j in range(KC):
                    act.activation(U_s[:, j, 4 * b:4 * b + 4, 0:CW - 1], ps[:, b, j * 120:(j + 1) * 120].rearrange("p (s t) -> p s t", s=4),
                                   ACT.Copy).then_inc(S_("us_state"), 1)
            act.wait_ge(S_("unat_done"), 1)
            act.activation(unat[:, 0, :], ps[:, 2, :], ACT.Copy).then_inc(S_("unat_evac0"), 1)
            act.activation(unat[0:NS, 1, :], ps[0:NS, 3, :], ACT.Copy).then_inc(S_("unat_evac"), 1)
            act.wait_ge(S_("unat_evac0"), 1)
            act.dma_start(out["conv_prompt"], unat[P - (CW - 1):P, 0, :]).then_inc(S_("unat_out"), 16)
            act.wait_ge(S_("unat_evac"), 1)
            act.dma_start(out["conv_sample"][0, :, CW - 1 - NEW:CW - 1, :], unat[0:NS, 1, :]).then_inc(S_("unat_out"), 16)
            def pexp(i):
                b = i // H
                nk = P * (b + 1)
                act.wait_ge(S_("plog_used"), i + 1)
                if i >= 4:
                    act.wait_ge(S_("pturn_done"), i - 3)
                act.activation(Pp[:, i % 4, 0:nk], Lp[:, i % 2, 0:nk], ACT.Exp, scale=-1.0, bias=small[:, 52 + i % 4:53 + i % 4],
                               accum_out=small[:, 56 + i % 4:57 + i % 4]).then_inc(S_("pexp_ready"), 1)

            def pevac(i):
                b = i // H
                act.wait_ge(S_("pturn_done"), i + 1)
                if i >= 2:
                    act.wait_ge(S_("patt_done"), i - 1)
                act.activation(pTp[:, i % 2, 0:b + 1, :], ps[:, 2 + i % 2, 0:P * (b + 1)].rearrange("p (a n) -> p a n", n=P), ACT.Copy)\
                    .then_inc(S_("pturn_evac"), 1)

            def pout(i):
                b, hp = i // 8, (i % 8) // 2
                act.wait_ge(S_("patt_done"), i + 1)
                act.activation(attT[:, hp, NS + P * b:NS + P * (b + 1)], ps[:, 6 + i // 2 % 2, 0:P], ACT.Copy).then_inc(S_("patt_evac"), 1)

            for i in range(35):
                if i < 32:
                    pexp(i)
                if 2 <= i <= 33:
                    pevac(i - 2)
                if i >= 3 and (i - 3) % 2 == 1:
                    pout(i - 3)
            act.wait_ge(S_("shift_ready"), 1)
            act.activation(L[:, :, :], L[:, :, :], ACT.Exp, scale=HD ** -0.5).then_inc(S_("exp_ready"), 1)
            act.wait_ge(S_("probsT_done"), 1)
            act.activation(pT[:, :, :, :], ps[:, 5:7, :].rearrange("p c (h q) -> p c h q", h=H), ACT.Copy).then_inc(S_("probsT_evac"), 1)
            act.activation(pnT[:, :, :], ps[0:NS, 7, :].rearrange("p (h q) -> p h q", h=H), ACT.Copy).then_inc(S_("probsT_evac"), 1)
            act.wait_ge(S_("probsT_evac"), 2)
            act.wait_ge(S_("zq_zero"), 1)
            with act.Fori(0, NS // 4) as i:
                for j in range(4):
                    act.wait_ge(S_("pv_used"), 4 * i + (j + 1))
                    act.activation(zq[:, j, :, 120:128], pT[:, :, :, bass.ds(4 * i + j, 1)].rearrange("p c h o -> p c (h o)"), ACT.Copy)\
                        .then_inc(S_("zq_ready"), 1)
            for k in range(KC):
                act.wait_ge(S_("xc_ready"), k + 1)
                act.activation(ysq[:, k, :], yacc[:, k, :], ACT.Square).then_inc(S_("ln_in"), 1)
            act.wait_ge(S_("lnvar_ready"), 1)
            act.activation(rstd[:, :], rstd[:, :], ACT.Sqrt).then_inc(S_("lnroot_ready"), 1)
            for k in range(KC):
                act.wait_ge(S_("z_ready"), k + 1)
                act.activation(yacc[:, k, :], yacc[:, k, :], ACT.Silu, bias=bcln[:, k:k + 1]).then_inc(S_("swish_ready"), 1)
            h0 = UM // 2
            for j in range(1, 9):
                split_hi(UM + j, j % 2, k=h0 + j // 2)
            for j in range(1, 9):
                split_hi(UO + j, j % 2, k=(UO + j) // 2)
            act.wait_ge(S_("o_free"), 2 + 4)
            squares(2)
            root(2)
            ffn(U2, C_FFN, 1)

        @block.vector
        def _(dve):
            own = [0]

            def link(ins):
                own[0] += 1
                ins.then_inc(S_("dve_own"), 1)
                return ins

            def settle():
                dve.wait_ge(S_("dve_own"), own[0])

            def lk(ins):
                link(ins)
                settle()

            def split_lo(u, slot, n=1024):
                dve.wait_ge(S_("hi_ready"), u + 1)
                dve.tensor_tensor(w_lo[:, slot, 0:n], w_raw[:, slot, 0:n], w_hi[:, slot, 0:n].bitcast(F32), ALU.subtract)\
                    .then_inc(S_("lo_ready"), 1)

            def norm(n, gain):
                dve.wait_ge(S_("sums_ready"), n + 1)
                dve.tensor_scalar(halves(rstd[:, :]), ps[:, 0:2, 0:HALF], 1.0 / D, EPS, ALU.mult, ALU.add).then_inc(S_("ms_ready"), 1)
                dve.wait_ge(S_("root_ready"), n + 1)
                lk(dve.reciprocal(rstd[:, :], rstd[:, :]))
                def low(k):
                    dve.wait_ge(S_("hhi_ready"), KD * n + k + 1)
                    dve.tensor_tensor(h_lo[:, k, :], hf[:, k % 3, :], h_hi[:, k, :].bitcast(F32), ALU.subtract).then_inc(S_("h_ready"), 1)

                for k in range(KD):
                    if k >= 3:
                        dve.wait_ge(S_("h_ready"), KD * n + k - 2)
                    dve.scalar_tensor_tensor(out=hf[:, k % 3, :], in0=xT[:, k, :], scalar=gain[:, k:k + 1], in1=rstd[:, :], op0=ALU.mult, op1=ALU.mult)\
                        .then_inc(S_("hf_ready"), 1)
                    if k:
                        low(k - 1)
                low(KD - 1)
                dve.wait_ge(S_("h_ready"), KD * (n + 1))

            def ffn(u0, f):
                with dve.Fori(0, FF // 256) as i:
                    for j in range(1, 5):
                        split_lo(4 * i + (u0 + j), j % 2)
                    dve.wait_ge(S_("unit_used"), 4 * i + (u0 + 6))
                    dve.wait_ge(S_("ping_free"), i + (C_FFN * f + 2))
                    for m in range(2):
                        dve.tensor_tensor(halves(prod_t[:, m, :]), halves(silu_g[:, m, :]), pair_ps(1, m), ALU.mult).then_inc(S_("prod_taken"), 1)
                    dve.wait_ge(S_("prod_taken"), 2 * i + (22 * f + 3))
                    dve.sem_inc(S_("pong_free"), 1)
                    for m in range(2):
                        dve.tensor_copy(a_hi[:, bass.ds(2 * i + m, 1), :].rearrange("p o n -> p (o n)"), prod_t[:, m, :]).then_inc(S_("ahi_ready"), 1)
                    dve.wait_ge(S_("ahi_ready"), 2 * i + (22 * f + 2))
                    for m in range(2):
                        dve.tensor_tensor(a_lo[:, bass.ds(2 * i + m, 1), :].rearrange("p o n -> p (o n)"), prod_t[:, m, :],
                                          a_hi[:, bass.ds(2 * i + m, 1), :].rearrange("p o n -> p (o n)").bitcast(F32), ALU.subtract)\
                            .then_inc(S_("act_ready"), 1)
                    dve.wait_ge(S_("act_ready"), 2 * i + (22 * f + 2))
                for i in range(2):
                    for half in range(2):
                        for j in range(6 * half + 1, 6 * half + 7):
                            if f == 0 or i == 0 or j < 12:
                                split_lo(12 * i + (u0 + 44 + j), j % 2, n=512 if j % 6 == 5 else 1024)
                        dve.wait_ge(S_("unit_used"), 12 * i + (u0 + 44 + 6 * half + 5 + 3))
                        for m in range(2):
                            xm = halves(xT[:, 4 * i + 2 * half + m, :])
                            ins = dve.scalar_tensor_tensor(out=xm, in0=pair_ps(half, m), scalar=0.5, in1=xm, op0=ALU.mult, op1=ALU.add)
                            ins.then_inc(S_("x_updated" if m == 0 else ("ping_free" if half == 0 else "pong_free")), 1)

            dve.sem_inc(S_("lo_ready"), 2)
            dve.sem_inc(S_("unit_used"), 2)
            dve.sem_inc(S_("ping_free"), 1)
            dve.sem_inc(S_("pong_free"), 1)
            dve.sem_inc(S_("kv_used"), 4)
            dve.sem_inc(S_("pv_used"), 4)
            dve.sem_inc(S_("mix_free"), 1)
            dve.sem_inc(S_("merge_free"), 2)
            dve.sem_inc(S_("o_free"), 2)
            for name in ("search", "prod_taken", "logits_ready", "mz_ready", "att_group", "m_ready"):
                dve.sem_inc(S_(name), 1)
            dve.memset(ones[:, :], 1.0).then_inc(S_("ones_ready"), 1)
            split_lo(0, 0)
            dve.wait_ge(S_("gain_in"), 16 * 14)
            dve.wait_ge(S_("xt_evac"), 2 * TB)
            norm(0, g1c)
            ffn(U1, 0)
            norm(1, gmc)

            dve.wait_ge(S_("rope_in"), 32)
            dve.wait_ge(S_("nat_evac"), TB)
            x = idxn[:, :, 0:288].rearrange("p b (h two d) -> p b h two d", two=2, d=16)
            ob = iro[:, :, 0:9, :].rearrange("p b h (two d) -> p b h two d", two=2)
            t1 = rt1[:, :, :, :].rearrange("p b h d -> p b (h d)")[:, :, 0:144].rearrange("p b (h d) -> p b h d", d=16)
            t2 = rt2[:, :, :, :].rearrange("p b h d -> p b (h d)")[:, :, 0:144].rearrange("p b (h d) -> p b h d", d=16)

            def rope(x1, x2, o1, o2, cos, sin, a, b):
                link(dve.tensor_tensor(a, x1, cos, ALU.mult))
                lk(dve.tensor_tensor(b, x2, sin, ALU.mult))
                lk(dve.tensor_tensor(a, a, b, ALU.subtract))
                link(dve.tensor_tensor(b, x1, sin, ALU.mult))
                lk(dve.tensor_tensor(x2, x2, cos, ALU.mult))
                link(dve.tensor_tensor(o2, b, x2, ALU.add))
                lk(dve.tensor_copy(o1, a))

            def bc(tab, c0, c1, nh):
                return tab[:, :, c0:c1].unsqueeze(2).to_broadcast([P, TB, nh, c1 - c0])

            rope(x[:, :, :, 0, :], x[:, :, :, 1, :], ob[:, :, :, 0, :], ob[:, :, :, 1, :],
                 bc(ropei, 0, 16, 9), bc(ropei, 16, 32, 9), t1, t2)
            link(dve.tensor_scalar(wisc[:, :, :], idxn[:, :, 288:296], IDX_SCALE, None, ALU.mult))
            dve.tensor_copy(iro[:, :, 9:12, :], iro[:, :, 8:9, :].to_broadcast([P, TB, 3, ID])).then_inc(S_("iro_ready"), 1)
            dve.wait_ge(S_("iro_ready"), 1)
            settle()
            dve.tensor_copy(qrep[:, :, :, :], iro[0:NS, 0, 0:8, :].unsqueeze(2).to_broadcast([NS, IH, 4, ID])).then_inc(S_("qrep_ready"), 1)
            n = 0
            for b in range(1, 4):
                nk = P * (b + 1)
                Sb = bias_new[:, b - 1, :]
                for h in range(IH):
                    dve.wait_ge(S_("prelu_ready"), n + 1)
                    w = wisc[:, b + 1, h:h + 1]
                    settle()
                    if n:
                        dve.wait_ge(S_("pscore_used"), n)
                    if h == 0:
                        dve.tensor_scalar(Sb[:, 0:nk], rp[:, n % 2, 0:nk], w, None, ALU.mult).then_inc(S_("pscore_used"), 1)
                    else:
                        dve.scalar_tensor_tensor(out=Sb[:, 0:nk], in0=rp[:, n % 2, 0:nk], scalar=w, in1=Sb[:, 0:nk], op0=ALU.mult, op1=ALU.add)\
                            .then_inc(S_("pscore_used"), 1)
                    n += 1
                dve.wait_ge(S_("pscore_used"), n)
                link(dve.tensor_tensor(Sb[:, P * b:nk], Sb[:, P * b:nk], causal[:, :], ALU.add))

            def choose(b):
                nk = P * (b + 1)
                Sb = bias_new[:, b - 1, 0:nk]
                for r in range(TOPK_P // 8):
                    lk(dve.max(m8[:, :], Sb))
                    lk(dve.match_replace(Sb, m8[:, :], Sb, TAKEN))
                dve.tensor_scalar(Sb, Sb, 2 * BARRED, OFF, ALU.is_ge, ALU.mult).then_inc(S_("choice_ready"), 1)

            choose(1)
            choose(2)
            choose(3)
            msq = small[:, 8:8 + TB * H]
            for w, (src, g) in enumerate(((qn, gqb), (kn, gkb))):
                dve.wait_ge(S_("nat_evac"), TB * (w + 2))
                v = src[:, :, :].rearrange("p b (h d) -> p (b h) d", d=HD)
                wk = rt1[:, :, :, :].rearrange("p b h d -> p (b h) d")
                for hh in range(2):
                    lk(dve.tensor_tensor(wk, v[:, :, 32 * hh:32 * hh + 32], v[:, :, 32 * hh:32 * hh + 32], ALU.mult))
                    lk(dve.tensor_reduce(msq if hh == 0 else rt2[:, 0, 0:2, :].rearrange("p a b -> p (a b)")[:, 0:TB * H], wk, AX.X, ALU.add))
                lk(dve.tensor_tensor(msq, msq, rt2[:, 0, 0:2, :].rearrange("p a b -> p (a b)")[:, 0:TB * H], ALU.add))
                dve.tensor_scalar(msq, msq, 1.0 / HD, EPS, ALU.mult, ALU.add).then_inc(S_("qkms_ready"), 1)
                dve.wait_ge(S_("qkroot_ready"), w + 1)
                lk(dve.reciprocal(msq, msq))
                lk(dve.tensor_tensor(v, v, msq.unsqueeze(2).to_broadcast([P, TB * H, HD]), ALU.mult))
                lk(dve.tensor_tensor(v, v, g[:, :].unsqueeze(1).to_broadcast([P, TB * H, HD]), ALU.mult))
                v4 = src[:, :, :].rearrange("p b (h two d) -> p b h two d", two=2, d=32)
                rope(v4[:, :, :, 0, :], v4[:, :, :, 1, :], v4[:, :, :, 0, :], v4[:, :, :, 1, :],
                     bc(ropet, 0, 32, H), bc(ropet, 32, 64, H), rt1[:, :, :, :], rt2[:, :, :, :])
                dve.sem_inc(S_("qk_ready"), 1)
            dve.wait_ge(S_("nat_stored"), 1)
            dve.wait_ge(S_("qkT_evac"), 2 * TB)
            lk(dve.memset(qbd[:, :, :, :], 0.0))
            dve.wait_ge(S_("qrepT_done"), 1)
            for k4 in range(4):
                r = 32 * k4
                dst = qbd[r:r + 32, :, k4 // 2, 64 * (k4 % 2):64 * (k4 % 2) + 64].rearrange("p s (q h) -> p s q h", q=8)
                link(dve.tensor_copy(dst, ps[r:r + 32, 4, :].rearrange("p (h s q) -> p s q h", h=IH, s=NSEQ)))
            dve.wait_ge(S_("wv_in"), 32)
            dve.wait_ge(S_("spread_in"), 16)
            for s in range(NSEQ):
                link(dve.tensor_scalar(wst[:, s, :], spread[:, s, :], wv[:, s:s + 1], None, ALU.mult))
            settle()
            dve.sem_inc(S_("qbd_ready"), 1)
            dve.wait_ge(S_("scores_done"), 4 * NSEQ)
            for half in range(2):
                dst = S[64 * half:64 * half + 64, 0:PAST // 2].rearrange("p (g k f) -> p k g f", g=16, f=4)
                for pr in range(2):
                    for k2 in range(2):
                        link(dve.tensor_copy(dst[:, :, :, 2 * pr + k2],
                                             ps[64 * k2:64 * k2 + 64, 2 * half + pr, :].rearrange("p (k g) -> p k g", g=16)))
            link(dve.memset(S[0:64, PAST // 2:WIDTH], BARRED))
            dve.wait_ge(S_("newdots_done"), 1)
            dve.wait_ge(S_("mask_in"), 32)
            nr = relud[0:NS, 0, :].rearrange("p (h k) -> p h k", h=IH)
            lk(dve.scalar_tensor_tensor(out=nr, in0=ps[0:NS, 6, :].rearrange("p (h k) -> p h k", h=IH), scalar=0.0,
                                        in1=wisc[0:NS, 0, :].unsqueeze(2).to_broadcast([NS, IH, NS]), op0=ALU.max, op1=ALU.mult))
            lk(dve.tensor_reduce(relud[0:NS, 1, 0:NS], nr.rearrange("p h k -> p k h"), AX.X, ALU.add))
            lk(dve.tensor_tensor(relud[0:NS, 1, 64:64 + NS], relud[0:NS, 1, 0:NS], newmask[:, :], ALU.add))
            lk(dve.tensor_copy(S[64:128, PAST // 2:WIDTH], relud[0:NS, 1, 64:64 + NS]))
            dve.sem_inc(S_("S_ready"), 1)
            def u_part(pr, m):
                ch = 2 * pr + m
                a = pair_ps(0, m)
                sg = halves(sgb[:, m, :])
                link(dve.tensor_tensor(U_s[:, ch, :, CW - 1:CW - 1 + NEW], sgb[:, m, 0:NS].rearrange("p (s t) -> p s t", s=NSEQ),
                                       a[:, 0, 0:NS].rearrange("p (s t) -> p s t", s=NSEQ), ALU.mult))
                link(dve.tensor_tensor(U_p[:, ch, CW - 1:CW - 1 + HALF - NS], sg[:, 0, NS:HALF], a[:, 0, NS:HALF], ALU.mult))
                dve.tensor_tensor(U_p[:, ch, CW - 1 + HALF - NS:CW - 1 + SEQ], sg[:, 1, :], a[:, 1, :], ALU.mult).then_inc(S_("u_ready"), 1)

            def u_pair(pr):
                dve.wait_ge(S_("sgb_ready"), pr + 1)
                dve.wait_ge(S_("mix_free"), 2 * pr + 2)
                dve.wait_ge(S_("unit_used"), UB + 4 * pr + 6)
                for m in range(2):
                    u_part(pr, m)
                dve.wait_ge(S_("u_ready"), 2 * pr + 2)
                dve.sem_inc(S_("mix_free"), 1)

            link(dve.memset(U_p[:, :, 0:CW - 1], 0.0))
            flip, cur, x_, bit, okay, msb = (ismall[:, n:n + 1] for n in range(6))

            def count(thr, op, dst):
                return dve.tensor_scalar(EQ[:, :], S[:, :], thr, 0.0, op, ALU.add, accum_out=dst)

            link(dve.memset(flip, -1))
            link(dve.memset(cur, 0))
            link(dve.memset(bit, 1 << 30))
            link(dve.memset(msb, -(1 << 31)))
            count(0.0, ALU.is_ge, small[:, 0:1]).then_inc(S_("cnt_ready"), 1)
            settle()
            dve.wait_ge(S_("tot_ready"), 1)
            lk(dve.tensor_scalar(okay, ps[:, 7, 0:1], float(TOPK_S), None, ALU.is_ge))
            link(dve.copy_predicated(flip, okay, msb))
            lk(dve.copy_predicated(cur, okay, msb))
            def search(first, last):
                with dve.Fori(first, last) as i:
                    dve.wait_ge(S_("search"), 4 * i + 1)
                    dve.scalar_tensor_tensor(out=x_, in0=cur, scalar=bit, in1=flip, op0=ALU.bitwise_or, op1=ALU.bitwise_xor).then_inc(S_("search"), 1)
                    dve.wait_ge(S_("search"), 4 * i + 2)
                    count(x_.bitcast(F32), ALU.is_ge, small[:, 0:1]).then_inc(S_("cnt_ready"), 1)
                    dve.wait_ge(S_("tot_ready"), i + 2)
                    dve.tensor_scalar(okay, ps[:, 7, 0:1], float(TOPK_S), -1.0, ALU.is_ge, ALU.mult).then_inc(S_("search"), 1)
                    dve.wait_ge(S_("search"), 4 * i + 3)
                    dve.scalar_tensor_tensor(out=cur, in0=okay, scalar=bit, in1=cur, op0=ALU.bitwise_and, op1=ALU.bitwise_or).then_inc(S_("search"), 1)
                    dve.wait_ge(S_("search"), 4 * i + 4)
                    dve.tensor_scalar(bit, bit, 1, None, ALU.logical_shift_right).then_inc(S_("search"), 1)

            search(0, 8)
            u_pair(0)
            search(8, 16)
            u_pair(1)
            search(16, 31)
            dve.wait_ge(S_("search"), 4 * 31 + 1)
            lk(dve.tensor_tensor(x_, cur, flip, ALU.bitwise_xor))
            thr = x_.bitcast(F32)
            lk(dve.tensor_scalar(SEL[:, :], S[:, :], thr, 0.0, ALU.is_gt, ALU.add, accum_out=small[:, 1:2]))
            count(thr, ALU.is_equal, small[:, 2:3]).then_inc(S_("cnt_ready"), 1)
            dve.wait_ge(S_("cnt_ready"), 33)
            link(dve.tensor_tensor_scan(CUM[:, :], EQ[:, :], EQ[:, :], 0.0, ALU.add, ALU.max))
            dve.wait_ge(S_("tot_ready"), 33)
            lk(dve.tensor_scalar(small[:, 3:4], ps[:, 7, 0:1], -1.0, float(TOPK_S), ALU.mult, ALU.add))
            lk(dve.scalar_tensor_tensor(out=EQ[:, :], in0=CUM[:, :], scalar=small[:, 3:4], in1=EQ[:, :], op0=ALU.is_le, op1=ALU.mult))
            dve.scalar_tensor_tensor(out=SEL[:, :], in0=SEL[:, :], scalar=1.0, in1=EQ[:, :], op0=ALU.mult, op1=ALU.add,
                                     accum_out=small[:, 4:5]).then_inc(S_("cnt_ready"), 1)
            dve.wait_ge(S_("tot_ready"), 34)
            dve.wait_ge(S_("cnt_ready"), 34)
            lk(dve.tensor_copy(small[:, 5:6], ps[:, 7, 0:1]))
            lk(dve.tensor_tensor_scan(CUM[:, :], SEL[:, :], SEL[:, :], small[:, 5:6], ALU.add, ALU.max))
            dve.tensor_tensor(CUM[:, :], CUM[:, :], SEL[:, :], ALU.mult).then_inc(S_("rank_ready"), 1)
            link(dve.tensor_scalar(nb[:, :], SEL[64:128, PAST // 2:WIDTH], -1.0, -OFF, ALU.add, ALU.mult))
            lk(dve.tensor_reduce(small[0:NS, 6:7], SEL[64:128, PAST // 2:WIDTH], AX.X, ALU.add))
            lk(dve.tensor_scalar(small[0:NS, 7:8], small[0:NS, 6:7], -1.0, float(TOPK_S), ALU.mult, ALU.add))
            link(dve.tensor_scalar(slotbias[:, :], slotno[:, :], small[0:NS, 7:8], OFF, ALU.is_ge, ALU.mult))
            for c4 in range(4):
                dve.wait_ge(S_("rankT_done"), c4 + 1)
                link(dve.tensor_scalar(RTi[:, 4 * c4:4 * c4 + 4, :], ps[:, c4, :].rearrange("p (c n) -> p c n", c=4), -1.0, None, ALU.add))
            settle()
            dve.sem_inc(S_("ranks_taken"), 1)
            lk(dve.tensor_scalar(tmpi[:, :, :], RTi[:, :, :], 4, None, ALU.arith_shift_right))
            lk(dve.tensor_copy(adig[:, :, :], tmpi[:, :, :]))
            lk(dve.tensor_scalar(tmpi[:, :, :], RTi[:, :, :], 15, None, ALU.bitwise_and))
            lk(dve.tensor_copy(bdig[:, :, :], tmpi[:, :, :]))
            dve.wait_ge(S_("tab_in"), 16 * 4)
            link(dve.tensor_copy(digit[:, :, :], digitf[:, :, :]))
            link(dve.tensor_scalar(ptv[:, 1, :], ptb[:, :], 1, None, ALU.arith_shift_right))
            lk(dve.tensor_scalar(ptv[:, 0, :], ptb[:, :], 1, 7, ALU.bitwise_and, ALU.logical_shift_left))
            lk(dve.tensor_scalar(ptv[:, 0, :], ptv[:, 0, :], pcol[:, 0:1], None, ALU.add))
            for v in range(2):
                link(dve.tensor_copy(tab[:, v, :, :, :].rearrange("p s g q -> p (s g) q"),
                                     ptv[:, v, :].unsqueeze(2).to_broadcast([P, NSEQ * NPAGE, 8])))
            settle()

            def own_slots(s):
                dve.wait_ge(S_("onehot_used"), 2 * s + 2)
                lk(dve.tensor_tensor(diag[:, :, :], ps[:, 5 + s % 2, 0:256].rearrange("p (x q) -> p x q", q=8), ownq[:, :, :], ALU.mult))
                lk(dve.tensor_reduce(rowidx[:, s, :], diag[:, :, :], AX.X, ALU.add))

            for s in range(NSEQ):
                for half in range(2):
                    if s:
                        dve.wait_ge(S_("onehot_used"), 2 * (s - 1) + half + 1)
                    pg = slice(16 * half, 16 * half + 16)
                    c0 = 64 * half + 8 * s
                    dg = digit[:, :, :].unsqueeze(1).to_broadcast([P, 16, 16, 8])
                    link(dve.tensor_tensor(ohA[:, pg, :, :], adig[:, :, c0:c0 + 8].unsqueeze(2).to_broadcast([P, 16, 16, 8]), dg, ALU.is_equal))
                    lk(dve.tensor_tensor(ohB[:, pg, :, :], bdig[:, :, c0:c0 + 8].unsqueeze(2).to_broadcast([P, 16, 16, 8]), dg, ALU.is_equal))
                    for v in range(2):
                        ins = dve.tensor_tensor(ohV[:, pg, v, :, :], ohB[:, pg, :, :], tab[:, v, s, pg, :].unsqueeze(2).to_broadcast([P, 16, 16, 8]), ALU.mult)
                        if v:
                            ins.then_inc(S_("onehot_ready"), 1)
                        else:
                            link(ins)
                if s:
                    own_slots(s - 1)
            own_slots(NSEQ - 1)
            dve.scalar_tensor_tensor(out=rowidx[:, :, 0:16], in0=rowidx[:, :, 16:32], scalar=256.0, in1=rowidx[:, :, 0:16],
                                     op0=ALU.mult, op1=ALU.add).then_inc(S_("rows_ready"), 1)
            dve.wait_ge(S_("idxT_done"), 1)
            dve.tensor_copy(idxT[:, :, :], ps[:, 6, 0:2 * NS].rearrange("p (c q) -> p c q", c=2)).then_inc(S_("idxT_ready"), 1)
            def key_logits(n, j):
                dve.wait_ge(S_(f"kv_in{j}"), 8 * (n - j) + 32)
                dve.wait_ge(S_(f"qb{j}"), 4 * (n - j) + 16)
                dve.wait_ge(S_("logits_ready"), n + 1)
                dve.tensor_tensor(kprod[:, :, :], kv[:, j, :, :], qb[:, j, :].unsqueeze(1).to_broadcast([P, 2, DA]), ALU.mult)\
                    .then_inc(S_("kv_used"), 1)
                dve.wait_ge(S_("kv_used"), n + 5)
                dve.tensor_reduce(G[:, :, bass.ds(n, 1)].rearrange("p c o -> p (c o)"),
                                  kprod[:, :, :].rearrange("p c (h d) -> p (c h) d", h=H), AX.X, ALU.add).then_inc(S_("logits_ready"), 1)

            def prompt_mask(b, n, t):
                nk = P * (b + 1)
                dve.wait_ge(S_("plog_done"), n + 1)
                dve.sem_inc(S_("mask_turn"), 1)
                bias = biasp[:, b - 1, 0:nk] if b else causal[:, :]
                dve.tensor_tensor_reduce(Lp[:, t % 2, 0:nk], ps[:, t % 2, 0:nk], bias, -HD ** -0.5, -TAKEN,
                                         ALU.add, ALU.min, small[:, 52 + t:53 + t]).then_inc(S_("plog_used"), 1)

            def prompt_quotient(b, n, t):
                nk = P * (b + 1)
                dve.wait_ge(S_("pexp_ready"), n + 1)
                dve.reciprocal(small[:, 60 + t:61 + t], small[:, 56 + t:57 + t]).then_inc(S_("pinv_ready"), 1)
                dve.wait_ge(S_("pinv_ready"), n + 1)
                dve.tensor_scalar(Pp[:, t, 0:nk], Pp[:, t, 0:nk], small[:, 60 + t:61 + t], None, ALU.mult)\
                    .then_inc(S_("pprob_ready"), 1)

            dve.wait_ge(S_("choice_back"), 48)
            for b in range(4):
                with dve.Fori(0, 2) as i:
                    for t in range(4):
                        prompt_mask(b, 4 * i + (H * b + t), t)
                        key_logits(8 * i + (16 * b + 2 * t), 2 * t % 4)
                        prompt_quotient(b, 4 * i + (H * b + t), t)
                        key_logits(8 * i + (16 * b + 2 * t + 1), 2 * t % 4 + 1)
            dve.wait_ge(S_("logitsT_done"), 1)
            link(dve.tensor_tensor(L[:, :, 0:TOPK_S], ps[0:NS, 0:4, :].rearrange("p b (h n) -> p (b h) n", h=2),
                                   slotbias[:, :].unsqueeze(1).to_broadcast([NS, H, TOPK_S]), ALU.add))
            lk(dve.tensor_tensor(L[:, :, TOPK_S:TOPK_S + NS], ps[0:NS, 4, :].rearrange("p (h n) -> p h n", h=H),
                                 nb[:, :].unsqueeze(1).to_broadcast([NS, H, NS]), ALU.add))
            mx, sm = small[0:NS, 8:16], small[0:NS, 16:24]
            lk(dve.tensor_reduce(mx, L[:, :, :], AX.X, ALU.max))
            dve.tensor_tensor(L[:, :, :], L[:, :, :], mx.unsqueeze(2).to_broadcast([NS, H, TOPK_S + NS]), ALU.subtract).then_inc(S_("shift_ready"), 1)
            dve.wait_ge(S_("exp_ready"), 1)
            lk(dve.tensor_reduce(sm, L[:, :, :], AX.X, ALU.add))
            lk(dve.reciprocal(sm, sm))
            dve.tensor_tensor(L[:, :, :], L[:, :, :], sm.unsqueeze(2).to_broadcast([NS, H, TOPK_S + NS]), ALU.mult).then_inc(S_("probs_ready"), 1)
            dve.wait_ge(S_("hm_in"), 32)

            def own_heads(g):
                dve.wait_ge(S_("pv_used"), 16 * g + 20)
                dve.wait_ge(S_("att_group"), g + 1)
                dve.tensor_tensor(mz[:, :], ps[:, 0, :], headmask[:, :], ALU.mult).then_inc(S_("mz_ready"), 1)

            ys = yacc[:, :, 0:NS].rearrange("p k (s t) -> p k s t", s=NSEQ)
            dve.wait_ge(S_("us_state"), 2 * KC)
            dve.wait_ge(S_("gate_saved"), 16 * 9)
            for j in range(CW):
                if j in (11, 22):
                    own_heads(j // 11 - 1)
                if j:
                    settle()
                for k in range(KC):
                    wj = wconv[:, k, j:j + 1]
                    if j == 0:
                        link(dve.tensor_scalar(yacc[:, k, NS:NT], U_p[:, k, 0:SEQ], wj, bconv[:, k:k + 1], ALU.mult, ALU.add))
                        link(dve.tensor_scalar(ys[:, k], U_s[:, k, :, 0:NEW], wj, bconv[:, k:k + 1], ALU.mult, ALU.add))
                    elif j < CW - 1:
                        link(dve.scalar_tensor_tensor(out=yacc[:, k, NS:NT], in0=U_p[:, k, j:j + SEQ], scalar=wj, in1=yacc[:, k, NS:NT], op0=ALU.mult, op1=ALU.add))
                        link(dve.scalar_tensor_tensor(out=ys[:, k], in0=U_s[:, k, :, j:j + NEW], scalar=wj, in1=ys[:, k], op0=ALU.mult, op1=ALU.add))
                    else:
                        link(dve.scalar_tensor_tensor(out=yacc[:, k, NS:NT], in0=U_p[:, k, j:j + SEQ], scalar=wj, in1=yacc[:, k, NS:NT], op0=ALU.mult, op1=ALU.add))
                        dve.scalar_tensor_tensor(out=ys[:, k], in0=U_s[:, k, :, j:j + NEW], scalar=wj, in1=ys[:, k], op0=ALU.mult, op1=ALU.add)\
                            .then_inc(S_("ln_in"), 1)
            own_heads(2)
            own_heads(3)
            dve.wait_ge(S_("att_group"), 5)
            lk(dve.tensor_copy(attT[:, :, 0:NS], ps[:, 4, 0:KA * NS].rearrange("p (k q) -> p k q", k=KA)))
            dve.tensor_tensor(attT[:, :, 0:NS], attT[:, :, 0:NS], ps[:, 5, 0:KA * NS].rearrange("p (k q) -> p k q", k=KA), ALU.add)\
                .then_inc(S_("atts_evac"), 1)
            dve.wait_ge(S_("ln_sums"), 1)
            mu = conv_mean[:, :]
            lk(dve.tensor_scalar(halves(mu), ps[:, 1:3, 0:HALF], 1.0 / DC, None, ALU.mult))
            for k in range(KC):
                dve.tensor_tensor(yacc[:, k, :], yacc[:, k, :], mu, ALU.subtract).then_inc(S_("xc_ready"), 1)
            dve.wait_ge(S_("ln_sums"), 2)
            dve.tensor_scalar(halves(rstd[:, :]), ps[:, 6:8, 0:HALF], 1.0 / DC, EPS, ALU.mult, ALU.add).then_inc(S_("lnvar_ready"), 1)
            dve.wait_ge(S_("lnvar_ready"), 1)
            dve.wait_ge(S_("lnroot_ready"), 1)
            lk(dve.reciprocal(rstd[:, :], rstd[:, :]))
            for k in range(KC):
                dve.scalar_tensor_tensor(out=yacc[:, k, :], in0=yacc[:, k, :], scalar=gcln[:, k:k + 1], in1=rstd[:, :], op0=ALU.mult, op1=ALU.mult)\
                    .then_inc(S_("z_ready"), 1)
            dve.wait_ge(S_("patt_evac"), 16)
            for k in range(KA):
                lk(dve.tensor_copy(t_hi[:, k, :], attT[:, k, :]))
                dve.tensor_tensor(t_lo[:, k, :], attT[:, k, :], t_hi[:, k, :].bitcast(F32), ALU.subtract).then_inc(S_("t_ready"), 1)
            dve.wait_ge(S_("gate_in0"), 16)
            dve.wait_ge(S_("gate_in1"), 16)
            with dve.Fori(0, 4) as i:
                dve.wait_ge(S_("unit_used"), 2 * i + (UM + 3))
                for m in range(2):
                    dve.tensor_tensor(halves(mc[:, m, :]), halves(gate_c[:, bass.ds(i, 1), m, :].rearrange("p o n -> p (o n)")), pair_ps(0, m), ALU.mult)\
                        .then_inc(S_("mc_part" if m == 0 else "merge_free"), 1)
                dve.wait_ge(S_("unit_used"), 2 * i + (UM + 4))
                ga = [gate_a[:, bass.ds(i, 1), m, :].rearrange("p o n -> p (o n)") for m in range(2)]
                for m in range(2):
                    dve.tensor_tensor(halves(ga[m]), halves(ga[m]), pair_ps(1, m), ALU.mult)\
                        .then_inc(S_("mc_part" if m == 0 else "merge_free"), 1)
                dve.wait_ge(S_("merge_free"), 2 * i + 4)
                dve.wait_ge(S_("mc_part"), 2 * i + 2)
                for m in range(2):
                    dve.tensor_tensor(mc[:, m, :], mc[:, m, :], ga[m], ALU.add).then_inc(S_("merge_step"), 1)
                dve.wait_ge(S_("merge_step"), 4 * i + 2)
                mh = [m_hi[:, bass.ds(2 * i + m, 1), :].rearrange("p o n -> p (o n)") for m in range(2)]
                ml = [m_lo[:, bass.ds(2 * i + m, 1), :].rearrange("p o n -> p (o n)") for m in range(2)]
                for m in range(2):
                    dve.tensor_copy(mh[m], mc[:, m, :]).then_inc(S_("merge_step"), 1)
                dve.wait_ge(S_("merge_step"), 4 * i + 4)
                for m in range(2):
                    dve.tensor_tensor(ml[m], mc[:, m, :], mh[m].bitcast(F32), ALU.subtract).then_inc(S_("m_ready"), 1)
                dve.wait_ge(S_("m_ready"), 2 * i + 3)
            dve.wait_ge(S_("lo_ready"), UO + 3)
            for pr in range(4):
                for j in (1, 2):
                    split_lo(UO + 2 * pr + j, j % 2)
                dve.wait_ge(S_("unit_used"), UO + 2 * pr + 4)
                for m in range(2):
                    xm = halves(xT[:, 2 * pr + m, :])
                    ins = dve.tensor_tensor(xm, xm, pair_ps(pr % 2, m), ALU.add)
                    ins.then_inc(S_("x_updated" if m == 0 else "o_free"), 1)
            norm(2, g2c)
            ffn(U2, 1)
            for f in range(2 * TB):
                n = NS if f < 2 else P
                dve.wait_ge(S_("y_done"), f + 1)
                dve.tensor_copy(xnat[0:n, f // 2, 512 * (f % 2):512 * (f % 2) + 512], ps[0:n, f % 2, :]).then_inc(S_("y_ready"), 1)

        @block.gpsimd
        def _(pool):
            def split_lo(u, slot, n):
                pool.wait_ge(S_("hi_ready"), u + 1)
                pool.tensor_tensor(w_lo[:, slot, 0:n], w_raw[:, slot, 0:n], w_hi[:, slot, 0:n].bitcast(F32), ALU.subtract)\
                    .then_inc(S_("lo_ready"), 1)

            pool.sem_inc(S_("gate_saved"), 16)
            pool.dma_start(out["conv_sample"][:, :, 0:CW - 1 - NEW, :], inp["state_conv"][:, :, NEW:CW - 1, :]).then_inc(S_("state_kept"), 16)
            pool.wait_ge(S_("ping_free"), C_FFN + 1)
            pool.wait_ge(S_("pong_free"), C_FFN + 1)
            pool.dma_start(ropet[:, :, :], con["rope"]).then_inc(S_("rope_in"), 16)
            pool.dma_start(ropei[:, :, :], con["ropei"]).then_inc(S_("rope_in"), 16)
            pool.wait_ge(S_("gain_in"), 16 * 14)
            ik_rows = inp["cache_idx_k"].rearrange("o n p d -> (o n) (p d)")
            pool.indirect_dma_start(ikn[:, :], None, ik_rows, bass.IndirectOffsetOnAxis(ap=ptile[:, 0:1], axis=0)).then_inc(S_("ik_in0"), 16)
            for name, dst, sem in (("pair", pairm, "sel_in"), ("first", firstm, "sel_in"), ("newmask", newmask, "mask_in"), ("slotno", slotno, "mask_in")):
                pool.dma_start(dst[:, :], con[name]).then_inc(S_(sem), 16)
            u = UA + 1
            for n in [2 * NI] * 3 + [2 * DA] * 12 + [1024]:
                split_lo(u, u % 2, n)
                u += 1
            pool.wait_ge(S_("iro_ready"), 1)
            pool.dma_start(wi_dram, wisc[0:NS, 0, :]).then_inc(S_("wi_saved"), 16)
            pool.wait_ge(S_("wi_saved"), 16)
            for k2 in range(2):
                pool.dma_start(wv[64 * k2:64 * k2 + 64, :], wi_dram.rearrange("(s q) h -> (q h) s", q=8), allow_slow_non_contiguous=True).then_inc(S_("wv_in"), 16)
            n_out = 0
            pool.wait_ge(S_("qk_ready"), 2)
            pool.wait_ge(S_("nat_evac"), 4 * TB)
            pool.dma_start(q_dram, qn[0:NS, 0, :]).then_inc(S_("q_saved"), 16)
            for tb in range(TB):
                n = NS if tb == 0 else P
                r0 = 0 if tb == 0 else P * (tb - 1)
                where = "sample" if tb == 0 else "prompt"
                for key, src in (("k_", kn[0:n, tb, :]), ("v_", vn[0:n, tb, :]), ("ik_", iro[0:n, tb, 8, :])):
                    pool.dma_start(out[key + where][r0:r0 + n], src).then_inc(S_("nat_out"), 16)
                    n_out += 1
            pool.wait_ge(S_("nat_out"), 16 * n_out)
            pool.wait_ge(S_("q_saved"), 16)
            pool.wait_ge(S_("qkT_evac"), 2 * TB)
            pool.wait_ge(S_("iT_evac"), TB)
            pool.wait_ge(S_("qrep_ready"), 1)
            pool.sem_inc(S_("nat_stored"), 1)
            pool.dma_start(spread[:, :, :], con["spread"]).then_inc(S_("spread_in"), 16)
            pool.dma_start(ptb[:, :], inp["page_table"].rearrange("(o s) n -> o (s n)", o=1).to_broadcast([P, NSEQ * NPAGE])).then_inc(S_("tab_in"), 16)
            pool.dma_start(digitf[:, :, :], con["digit"]).then_inc(S_("tab_in"), 16)
            pool.dma_start(pcol[:, :], con["pcol"]).then_inc(S_("tab_in"), 16)
            pool.wait_ge(S_("ikT_evac"), 8)
            pool.indirect_dma_start(ikn[:, :], None, ik_rows, bass.IndirectOffsetOnAxis(ap=ptile[:, 1:2], axis=0)).then_inc(S_("ik_in1"), 16)
            pool.wait_ge(S_("choice_saved"), 48)
            pool.dma_start(ownq[:, :, :], con["ownq"]).then_inc(S_("tab_in"), 16)
            for u in range(UB + 1, UM):
                split_lo(u, u % 2, 1024)
            pool.wait_ge(S_("rows_ready"), 1)
            pool.dma_start(headmask[:, :], con["headmask"]).then_inc(S_("hm_in"), 16)
            pool.dma_start(qsel[:, :], con["qsel"]).then_inc(S_("hm_in"), 16)
            pool.dma_start(idx_dram.rearrange("a q s b -> (a q) s b"), rowidx[:, :, 0:16]).then_inc(S_("idx_saved"), 16)
            pool.wait_ge(S_("idx_saved"), 16)
            for s in range(NSEQ):
                pool.dma_start(idxr[8 * s:8 * s + 8, :].rearrange("q (a b) -> q a b", b=16), idx_dram[:, :, s, :].rearrange("a q b -> q a b"))\
                    .then_inc(S_("idx_back"), 16)
            for b in range(2):
                pool.dma_start(stn[:, b, :], inp["state_conv"][0, 4 * b:4 * b + 4].rearrange("s t c -> (s t) c")).then_inc(S_("state_in"), 16)
            pool.wait_ge(S_("idxT_ready"), 1)
            for w, name in enumerate(("cache_k", "cache_v")):
                rows = inp[name].rearrange("o n p h d -> (o n p) (h d)")
                if w == 1:
                    pool.wait_ge(S_("kv_used"), NS + 4)
                    pool.wait_ge(S_("pturn_done"), 32)
                    pool.memset(zq[:, :, :, :], 0.0).then_inc(S_("zq_zero"), 1)
                with pool.Fori(0, NS // 4) as i:
                    for j in range(4):
                        pool.wait_ge(S_("pv_used" if w else "kv_used"), 4 * i + (j + 1))
                        pool.tensor_copy(slotidx[:, j, :], idxT[:, :, bass.ds(4 * i + j, 1)].rearrange("p c o -> p (c o)")).then_inc(S_("slot_set"), 1)
                        pool.wait_ge(S_("slot_set"), 4 * i + (NS * w + j + 1))
                        pool.sem_inc(S_("gather_turn"), 1)
                        for c in range(2):
                            pool.indirect_dma_start(kv[:, j, c, :], None, rows, bass.IndirectOffsetOnAxis(ap=slotidx[:, j, c:c + 1], axis=0))\
                                .then_inc(S_(f"kv_in{j}"), 16)
            gates = gate_dram.rearrange("(g i) p n -> g p i n", g=2)
            pool.wait_ge(S_("ln_in"), KC)
            pool.wait_ge(S_("lnvar_ready"), 1)
            pool.dma_start(gate_c[:, :, :, :].rearrange("p i m n -> p i (m n)"), gates[0]).then_inc(S_("gate_in0"), 16)
            for k in range(KC):
                pool.wait_ge(S_("swish_ready"), k + 1)
                pool.tensor_copy(c_hi[:, k, :], yacc[:, k, :]).then_inc(S_("chi_ready"), 1)
                pool.wait_ge(S_("chi_ready"), k + 1)
                pool.tensor_tensor(c_lo[:, k, :], yacc[:, k, :], c_hi[:, k, :].bitcast(F32), ALU.subtract).then_inc(S_("c_ready"), 1)
            for u in range(UM, UO + 1):
                if u == UM + 1:
                    pool.wait_ge(S_("t_ready"), KA)
                    pool.dma_start(gate_a[:, :, :, :].rearrange("p i m n -> p i (m n)"), gates[1]).then_inc(S_("gate_in1"), 16)
                split_lo(u, u % 2, 1024)
            pool.wait_ge(S_("state_kept"), 16)
            pool.wait_ge(S_("unat_out"), 32)


_IN = ["x_prompt", "x_sample", "cache_k", "cache_v", "cache_idx_k", "state_conv", "page_table", "g_ffn1", "w_ffn1_in",
       "w_ffn1_out", "g_mix", "w_in", "g_q", "g_k", "w_dw", "b_dw", "g_cln", "b_cln", "w_cout", "w_aout", "w_o",
       "g_ffn2", "w_ffn2_in", "w_ffn2_out"]
_OUT = [("y_prompt", (SEQ, D), (1, SEQ, D)), ("y_sample", (NS, D), (NSEQ, NEW, D)),
        ("k_prompt", (SEQ, DA), (1, 1, SEQ, H, HD)), ("v_prompt", (SEQ, DA), (1, 1, SEQ, H, HD)),
        ("ik_prompt", (SEQ, ID), (1, 1, SEQ, ID)), ("conv_prompt", (CW - 1, DC), (1, 1, CW - 1, DC)),
        ("k_sample", (NS, DA), (1, NSEQ, NEW, H, HD)), ("v_sample", (NS, DA), (1, NSEQ, NEW, H, HD)),
        ("ik_sample", (NS, ID), (1, NSEQ, NEW, ID)), ("conv_sample", (1, NSEQ, CW - 1, DC), (1, NSEQ, CW - 1, DC))]


def kernel(**inputs):
    import concourse.bacc as bacc
    from concourse.bass_utils import run_bass_kernel_spmd

    nc = bacc.Bacc("TRN2", target_bir_lowering=False, num_devices=1)
    arrays, inp, con, out = {}, {}, {}, {}
    for name in _IN:
        a = np.ascontiguousarray(inputs[name])
        if name in ("x_prompt", "x_sample"):
            a = a.reshape(-1, D)
        arrays[name] = a
        inp[name] = nc.dram_tensor(name, a.shape, mybir.dt.from_np(a.dtype), kind="ExternalInput").ap()
    for name, a in constants().items():
        arrays["c_" + name] = a
        con[name] = nc.dram_tensor("c_" + name, a.shape, F32, kind="ExternalInput").ap()
    for name, shape, _ in _OUT:
        out[name] = nc.dram_tensor("o_" + name, shape, F32, kind="ExternalOutput").ap()
    hybrid_step(nc, inp, con, out)
    r = run_bass_kernel_spmd(nc, [arrays], core_ids=[0])
    return tuple(r.results[0]["o_" + name].reshape(shape) for name, _, shape in _OUT)
```
